# Optimizing a Trainium2 kernel written in Bass

```python
import jax, jax.numpy as jnp
from jax import lax
import numpy as np
import jax
import jax.numpy as jnp
import math

D_MODEL = 1024
BATCH = 1
SEQ = 256
DEPTH = 1

CTX_LEN = 256
GRID_W = 64
D_FOURIER = D_MODEL // 2
FOURIER_GROUPS = 4
FOURIER_GROUP_DIM = D_FOURIER // FOURIER_GROUPS
D_REC = D_MODEL - D_FOURIER
REC_HEADS = 4
REC_HEAD_DIM = D_REC // REC_HEADS
CHUNK = 64
SUB_CHUNK = 16
N_EXPERTS = 16
EC_CAPACITY_FACTOR = 2
D_EXPERT = 2816
NORM_EPS = 1e-6
D_IN = D_FOURIER + 5 * D_REC
N_ADA = 6


def rms_norm(x, gain):
    xf = x.astype(jnp.float32)
    y = xf * lax.rsqrt(jnp.mean(xf * xf, axis=-1, keepdims=True) + NORM_EPS)
    return (y * gain.astype(jnp.float32)).astype(x.dtype)

def adaln(cond, w, b):
    mod = (jax.nn.silu(cond) @ w + b)[:, None, :]
    return jnp.split(mod, N_ADA, axis=-1)

def modulate(h, shift, scale):
    return h * (1 + scale) + shift

def fourier_mix(u, w_f):
    b_, l_, _ = u.shape
    z = u.astype(jnp.float32).reshape(b_, l_, FOURIER_GROUPS, FOURIER_GROUP_DIM)
    z = jnp.fft.fft2(z, axes=(1, 3), norm="ortho").real.astype(u.dtype)
    y = jnp.einsum('blgc,gcd->blgd', z, w_f)
    return y.reshape(b_, l_, D_FOURIER)

def _to_chunks(t):
    b_, l_, h_, d_ = t.shape
    return t.reshape(b_, l_ // CHUNK, CHUNK, h_, d_).transpose(1, 0, 3, 2, 4)

def _from_chunks(t):
    n_, b_, h_, c_, d_ = t.shape
    return t.transpose(1, 0, 3, 2, 4).reshape(b_, n_ * c_, h_, d_)

def _chunk_step(S, inp):
    qc, kc, vc, lc = inp
    b_, h_, c_, d_ = qc.shape
    ns = c_ // SUB_CHUNK
    bcum = jnp.cumsum(lc, axis=2)
    o_inter = jnp.einsum('bhcd,bhde->bhce', qc * jnp.exp(bcum), S)
    bs = bcum.reshape(b_, h_, ns, SUB_CHUNK, d_)
    qs = qc.reshape(b_, h_, ns, SUB_CHUNK, d_)
    ks = kc.reshape(b_, h_, ns, SUB_CHUNK, d_)
    vs = vc.reshape(b_, h_, ns, SUB_CHUNK, -1)
    b_ref = jnp.concatenate([jnp.zeros_like(bs[:, :, :1, 0]), bs[:, :, :-1, -1]], axis=2)
    q_hat = qs * jnp.exp(bs - b_ref[:, :, :, None, :])
    prev = jnp.arange(c_)[None, :] < (jnp.arange(ns) * SUB_CHUNK)[:, None]
    k_hat = kc[:, :, None] * jnp.exp(jnp.where(prev[:, :, None],
                                               b_ref[:, :, :, None, :] - bcum[:, :, None], -jnp.inf))
    a_off = jnp.einsum('bhjtd,bhjsd->bhjts', q_hat, k_hat)
    tri = jnp.tril(jnp.ones((SUB_CHUNK, SUB_CHUNK), dtype=bool))
    decay = jnp.exp(jnp.where(tri[:, :, None],
                              bs[:, :, :, :, None, :] - bs[:, :, :, None, :, :], -jnp.inf))
    a_diag = jnp.einsum('bhjtd,bhjtsd,bhjsd->bhjts', qs, decay, ks)
    o_intra = (jnp.einsum('bhjts,bhse->bhjte', a_off, vc)
               + jnp.einsum('bhjts,bhjse->bhjte', a_diag, vs))
    o = o_inter + o_intra.reshape(b_, h_, c_, -1)
    b_last = bcum[:, :, -1]
    S_new = (jnp.exp(b_last)[..., None] * S
             + jnp.einsum('bhcd,bhce->bhde', kc * jnp.exp(b_last[:, :, None] - bcum), vc))
    return S_new, o

def scan_dir(q, k, v, logf, S0, reverse):
    if reverse:
        q, k, v, logf = (jnp.flip(t, axis=1) for t in (q, k, v, logf))
    S_fin, o = lax.scan(_chunk_step, S0, (_to_chunks(q), _to_chunks(k), _to_chunks(v), _to_chunks(logf)))
    o = _from_chunks(o)
    if reverse:
        o = jnp.flip(o, axis=1)
    return o, S_fin

def split_proj(p, lb):
    b_, l_, _ = p.shape
    u, q, v, f_f, f_b, g = jnp.split(p, [D_FOURIER + i * D_REC for i in range(5)], axis=-1)
    heads = lambda t: t.astype(jnp.float32).reshape(b_, l_, REC_HEADS, REC_HEAD_DIM)

    def gates(fp, lbd):
        lbd = lbd.reshape(REC_HEADS, REC_HEAD_DIM)
        fg = lbd + (1 - lbd) * jax.nn.sigmoid(heads(fp))
        return jnp.log(fg), 1 - fg

    return u, jax.nn.silu(heads(q)), heads(v), gates(f_f, lb[0]), gates(f_b, lb[1]), g

def rec_mixer(q, v, gf, gb, g, S0_f, S0_b, gain):
    o_f, S_f = scan_dir(q, gf[1], v, gf[0], S0_f, False)
    o_b, S_b = scan_dir(q, gb[1], v, gb[0], S0_b, True)
    o = o_f + o_b
    o = o * lax.rsqrt(jnp.mean(o * o, axis=-1, keepdims=True) + NORM_EPS)
    o = o * gain.astype(jnp.float32).reshape(REC_HEADS, REC_HEAD_DIM)
    b_, l_ = o.shape[:2]
    y = o.reshape(b_, l_, D_REC).astype(g.dtype) * jax.nn.silu(g)
    return y, S_f, S_b

def ec_moe(h, w_r, w_g, w_u, w_d):
    b_, l_, d_ = h.shape
    cap = EC_CAPACITY_FACTOR * l_ // N_EXPERTS
    affinity = jax.nn.softmax((h @ w_r).astype(jnp.float32), axis=-1)
    gate, idx = lax.top_k(jnp.swapaxes(affinity, 1, 2), cap)
    xs = jax.vmap(lambda hb, ib: hb[ib])(h, idx)
    hid = jax.nn.silu(jnp.einsum('becd,edf->becf', xs, w_g)) * jnp.einsum('becd,edf->becf', xs, w_u)
    ye = jnp.einsum('becf,efd->becd', hid, w_d) * gate[..., None].astype(h.dtype)
    flat = (idx + jnp.arange(b_)[:, None, None] * l_).reshape(-1)
    out = jax.ops.segment_sum(ye.reshape(-1, d_), flat, num_segments=b_ * l_)
    return out.reshape(b_, l_, d_)

def first_inputs(seed: int = 0) -> dict:
    key = jax.random.key(seed)
    ks = jax.random.split(key, 20)
    nrm = lambda k, shape, s: jax.random.normal(k, shape, jnp.float32) * s
    D = D_MODEL
    return {
        "x": nrm(ks[0], (BATCH, SEQ, D), 1.0),
        "c": nrm(ks[1], (BATCH, D), 1.0),
        "ctx": nrm(ks[2], (BATCH, CTX_LEN, D), 1.0),
        "c_ctx": nrm(ks[3], (D,), 1.0),
        "w_ada": nrm(ks[4], (DEPTH, D, N_ADA * D), 0.5 * D ** -0.5),
        "b_ada": nrm(ks[5], (DEPTH, N_ADA * D), 0.01),
        "g_mix": 1.0 + nrm(ks[6], (DEPTH, D), 0.02),
        "w_in": nrm(ks[7], (DEPTH, D, D_IN), D ** -0.5),
        "w_fourier": nrm(ks[8], (DEPTH, FOURIER_GROUPS, FOURIER_GROUP_DIM, FOURIER_GROUP_DIM), FOURIER_GROUP_DIM ** -0.5),
        "lb_logits": nrm(ks[9], (DEPTH + 1, 2, D_REC), 0.5),
        "g_rec": 1.0 + nrm(ks[10], (DEPTH, D_REC), 0.02),
        "w_out": nrm(ks[11], (DEPTH, D, D), D ** -0.5),
        "g_ffn": 1.0 + nrm(ks[12], (DEPTH, D), 0.02),
        "w_router": nrm(ks[13], (DEPTH, D, N_EXPERTS), D ** -0.5),
        "w_exp_gate": nrm(ks[14], (DEPTH, N_EXPERTS, D, D_EXPERT), D ** -0.5),
        "w_exp_up": nrm(ks[15], (DEPTH, N_EXPERTS, D, D_EXPERT), D ** -0.5),
        "w_exp_down": nrm(ks[16], (DEPTH, N_EXPERTS, D_EXPERT, D), D_EXPERT ** -0.5),
        "g_final": 1.0 + nrm(ks[17], (D,), 0.02),
    }

def first_block(x, c, ctx, c_ctx, w_ada, b_ada, g_mix, w_in, w_fourier, lb_logits, g_rec, w_out,
              g_ffn, w_router, w_exp_gate, w_exp_up, w_exp_down, g_final):
    b_ = x.shape[0]
    lb_all = jnp.cumsum(jax.nn.softmax(lb_logits.astype(jnp.float32), axis=0), axis=0)
    for layer in range(DEPTH):
        ctx_out_needed = layer < DEPTH - 1
        sh1, sc1, gt1, sh2, sc2, gt2 = adaln(c, w_ada[layer], b_ada[layer])
        sh1c, sc1c, gt1c, sh2c, sc2c, gt2c = adaln(c_ctx[None], w_ada[layer], b_ada[layer])
        lb = lb_all[layer]

        h_ctx = modulate(rms_norm(ctx, g_mix[layer]), sh1c, sc1c)
        h_lat = modulate(rms_norm(x, g_mix[layer]), sh1, sc1)
        u_c, q_c, v_c, gf_c, gb_c, g_c = split_proj(h_ctx @ w_in[layer], lb)
        u_l, q_l, v_l, gf_l, gb_l, g_l = split_proj(h_lat @ w_in[layer], lb)

        S_zero = jnp.zeros((b_, REC_HEADS, REC_HEAD_DIM, REC_HEAD_DIM), jnp.float32)
        rec_c, S_cf, S_cb = rec_mixer(q_c, v_c, gf_c, gb_c, g_c, S_zero, S_zero, g_rec[layer])
        rec_l, _, _ = rec_mixer(q_l, v_l, gf_l, gb_l, g_l, S_cf, S_cb, g_rec[layer])

        mix_l = jnp.concatenate([fourier_mix(u_l, w_fourier[layer]), rec_l], axis=-1) @ w_out[layer]
        x = x + gt1 * mix_l
        if ctx_out_needed:
            mix_c = jnp.concatenate([fourier_mix(u_c, w_fourier[layer]), rec_c], axis=-1) @ w_out[layer]
            ctx = ctx + gt1c * mix_c

        x = x + gt2 * ec_moe(modulate(rms_norm(x, g_ffn[layer]), sh2, sc2), w_router[layer],
                             w_exp_gate[layer], w_exp_up[layer], w_exp_down[layer])
        if ctx_out_needed:
            ctx = ctx + gt2c * ec_moe(modulate(rms_norm(ctx, g_ffn[layer]), sh2c, sc2c), w_router[layer],
                                      w_exp_gate[layer], w_exp_up[layer], w_exp_down[layer])
    return rms_norm(x, g_final)


HEAD_DIM = 64
N_ATTN_HEADS = (D_MODEL // 2) // HEAD_DIM
ATTN_WIDTH = N_ATTN_HEADS * HEAD_DIM
MOBA_BLOCK = 256
MOBA_TOPK = 3
Q_CHUNK = 128
SGU_WIDTH = D_MODEL // 2
N_SGU_GROUPS = 8
SGU_GROUP_DIM = SGU_WIDTH // N_SGU_GROUPS
SGU_CHUNK = 128
D_FF = 4 * D_MODEL
N_MOD = 6
IN_WIDTH = 3 * ATTN_WIDTH + 2 * SGU_WIDTH + 2 * D_MODEL
EPS = 1e-6


def rmsnorm(x, g):
    xf = x.astype(jnp.float32)
    y = xf * lax.rsqrt(jnp.mean(xf * xf, axis=-1, keepdims=True) + EPS)
    return (y * g.astype(jnp.float32)).astype(x.dtype)

def moba_attention(q, k, v):
    B, S, H, Dh = q.shape
    L = MOBA_BLOCK
    nb = -(-S // L)
    s_pad = nb * L
    nqc = S // Q_CHUNK
    k_sel = min(MOBA_TOPK, nb - 1)
    scale = Dh ** -0.5
    qh = q.transpose(0, 2, 1, 3)
    pad = ((0, 0), (0, 0), (0, s_pad - S), (0, 0))
    kb = jnp.pad(k.transpose(0, 2, 1, 3), pad).reshape(B, H, nb, L, Dh)
    vb = jnp.pad(v.transpose(0, 2, 1, 3), pad).reshape(B, H, nb, L, Dh)
    qblk = jnp.arange(S) // L
    if k_sel > 0:
        kmean = jnp.mean(kb.astype(jnp.float32), axis=3)
        gate = jnp.einsum('bhsd,bhnd->bhsn', qh.astype(jnp.float32), kmean)
        fully_past = jnp.arange(nb)[None, :] < qblk[:, None]
        gate = jnp.where(fully_past[None, None], gate, -jnp.inf)
        _, idx = lax.top_k(gate, k_sel)
    else:
        idx = jnp.zeros((B, H, S, 0), jnp.int32)
    valid = idx < qblk[None, None, :, None]

    def to_chunks(a):
        tail = a.shape[3:]
        a = a.reshape((B, H, nqc, Q_CHUNK) + tail).swapaxes(1, 2)
        return a.reshape((B * nqc, H, Q_CHUNK) + tail)

    q_c = to_chunks(qh)
    idx_c = to_chunks(idx)
    valid_c = to_chunks(valid)
    b_ids = jnp.repeat(jnp.arange(B, dtype=jnp.int32), nqc)
    c_ids = jnp.tile(jnp.arange(nqc, dtype=jnp.int32), B)
    heads = jnp.arange(H)[:, None, None]
    offs_q = jnp.arange(Q_CHUNK)
    offs_k = jnp.arange(L)

    def attend_chunk(args):
        qi, ii, vi, bi, ci = args
        kb_b = lax.dynamic_index_in_dim(kb, bi, 0, keepdims=False)
        vb_b = lax.dynamic_index_in_dim(vb, bi, 0, keepdims=False)
        blk = (ci * Q_CHUNK) // L
        k_own = lax.dynamic_index_in_dim(kb_b, blk, 1, keepdims=False)
        v_own = lax.dynamic_index_in_dim(vb_b, blk, 1, keepdims=False)
        qf = qi.astype(jnp.float32) * scale
        s_own = jnp.einsum('hqd,hld->hql', qf, k_own.astype(jnp.float32))
        causal = (blk * L + offs_k)[None, :] <= (ci * Q_CHUNK + offs_q)[:, None]
        s_own = jnp.where(causal[None], s_own, -jnp.inf)
        k_g = kb_b[heads, ii]
        v_g = vb_b[heads, ii]
        s_g = jnp.einsum('hqd,hqkld->hqkl', qf, k_g.astype(jnp.float32))
        s_g = jnp.where(vi[..., None], s_g, -jnp.inf).reshape(H, Q_CHUNK, k_sel * L)
        p = jax.nn.softmax(jnp.concatenate([s_own, s_g], axis=-1), axis=-1)
        p_own = p[..., :L]
        p_g = p[..., L:].reshape(H, Q_CHUNK, k_sel, L)
        o = (jnp.einsum('hql,hld->hqd', p_own, v_own.astype(jnp.float32))
             + jnp.einsum('hqkl,hqkld->hqd', p_g, v_g.astype(jnp.float32)))
        return o.astype(qi.dtype)

    o = lax.map(attend_chunk, (q_c, idx_c, valid_c, b_ids, c_ids))
    o = o.reshape(B, nqc, H, Q_CHUNK, Dh).transpose(0, 1, 3, 2, 4)
    return o.reshape(B, S, H * Dh)

def spatial_gating(u, vs, g_v, w_s, b_s):
    B, S, _ = u.shape
    nc = S // SGU_CHUNK
    vs = rmsnorm(vs, g_v)
    vg = vs.reshape(B, nc, SGU_CHUNK, N_SGU_GROUPS, SGU_GROUP_DIM)
    w_causal = jnp.tril(w_s)
    z = jnp.einsum('gts,bcsgd->bctgd', w_causal, vg) + b_s.T[None, None, :, :, None]
    return u * z.reshape(B, S, SGU_WIDTH)

def second_inputs(seed: int = 0) -> dict:
    key = jax.random.key(seed)
    ks = jax.random.split(key, 16)
    f32 = jnp.float32
    nrm = lambda k, shape, s: jax.random.normal(k, shape, f32) * s
    return {
        "x": nrm(ks[0], (BATCH, SEQ, D_MODEL), 1.0),
        "c": nrm(ks[1], (BATCH, D_MODEL), 1.0),
        "w_ada": nrm(ks[2], (DEPTH, D_MODEL, N_MOD * D_MODEL), 0.5 * D_MODEL ** -0.5),
        "b_ada": nrm(ks[3], (DEPTH, N_MOD * D_MODEL), 0.01),
        "g_mix": 1.0 + nrm(ks[4], (DEPTH, D_MODEL), 0.01),
        "w_in": nrm(ks[5], (DEPTH, D_MODEL, IN_WIDTH), D_MODEL ** -0.5),
        "w_proj_attn": nrm(ks[6], (DEPTH, ATTN_WIDTH, D_MODEL), ATTN_WIDTH ** -0.5),
        "g_sgu": 1.0 + nrm(ks[7], (DEPTH, SGU_WIDTH), 0.01),
        "w_sgu": nrm(ks[8], (DEPTH, N_SGU_GROUPS, SGU_CHUNK, SGU_CHUNK), SGU_CHUNK ** -0.5),
        "b_sgu": 1.0 + nrm(ks[9], (DEPTH, N_SGU_GROUPS, SGU_CHUNK), 0.01),
        "w_proj_sgu": nrm(ks[10], (DEPTH, SGU_WIDTH, D_MODEL), SGU_WIDTH ** -0.5),
        "w_out": nrm(ks[11], (DEPTH, D_MODEL, D_MODEL), D_MODEL ** -0.5),
        "g_ffn": 1.0 + nrm(ks[12], (DEPTH, D_MODEL), 0.01),
        "w_ff1": nrm(ks[13], (DEPTH, D_MODEL, D_FF), D_MODEL ** -0.5),
        "w_ff2": nrm(ks[14], (DEPTH, D_FF, D_MODEL), D_FF ** -0.5),
        "g_final": 1.0 + nrm(ks[15], (D_MODEL,), 0.01),
    }

def second_block(x, c, w_ada, b_ada, g_mix, w_in, w_proj_attn, g_sgu, w_sgu, b_sgu,
              w_proj_sgu, w_out, g_ffn, w_ff1, w_ff2, g_final):
    B, S, _ = x.shape
    A, W, D = ATTN_WIDTH, SGU_WIDTH, D_MODEL
    splits = [A, 2 * A, 3 * A, 3 * A + W, 3 * A + 2 * W, 3 * A + 2 * W + D]
    c_act = jax.nn.silu(c)
    for l in range(DEPTH):
        mod = (c_act @ w_ada[l] + b_ada[l])[:, None, :]
        shift1, scale1, gate1, shift2, scale2, gate2 = jnp.split(mod, N_MOD, axis=-1)
        h = rmsnorm(x, g_mix[l]) * (1 + scale1) + shift1
        proj = h @ w_in[l]
        q, k, v, u, vs, ga, gb = jnp.split(proj, splits, axis=-1)
        hs = (B, S, N_ATTN_HEADS, HEAD_DIM)
        y_attn = moba_attention(q.reshape(hs), k.reshape(hs), v.reshape(hs)) @ w_proj_attn[l]
        y_sgu = spatial_gating(jax.nn.gelu(u), jax.nn.gelu(vs), g_sgu[l], w_sgu[l], b_sgu[l]) @ w_proj_sgu[l]
        merged = jax.nn.sigmoid(ga) * y_attn + jax.nn.sigmoid(gb) * y_sgu
        x = x + gate1 * (merged @ w_out[l])
        h = rmsnorm(x, g_ffn[l]) * (1 + scale2) + shift2
        x = x + gate2 * (jnp.square(jax.nn.relu(h @ w_ff1[l])) @ w_ff2[l])
    return rmsnorm(x, g_final)


_first_inputs = second_inputs


def second_inputs(seed=0):
    import zlib

    import numpy as np

    out = dict(_first_inputs(seed))
    spreads = {}
    factors = {'b_ada': 3.749, 'g_mix': 8.0, 'g_sgu': 8.0, 'b_sgu': 8.0, 'g_ffn': 8.0, 'g_final': 5.676}
    for name, (base, spread) in spreads.items():
        noise = np.random.default_rng([zlib.crc32(name.encode()), seed]).standard_normal(out[name].shape)
        drawn = base * np.exp(spread * noise) if base else spread * noise
        out[name] = jnp.asarray(drawn.astype(out[name].dtype))
    for name, factor in factors.items():
        out[name] = (out[name] * factor).astype(out[name].dtype)
    return out


_narrow_inputs = second_inputs


def second_inputs(seed=0):

    out = dict(_narrow_inputs(seed))
    wider = {'g_sgu': 10.09, 'b_sgu': 7.06, 'g_ffn': 6.21, 'g_final': 6.26}
    for name, times in wider.items():
        mean = out[name].mean()
        out[name] = (mean + times * (out[name] - mean)).astype(out[name].dtype)
    return out


DEPTH_3 = 2

N_ATT_HEADS = 8
ATT_WIDTH = N_ATT_HEADS * HEAD_DIM
N_CONV_GROUPS = 8
CONV_WIDTH = 512
MIX_WIDTH = ATT_WIDTH + CONV_WIDTH
IN_COLS = 4 * ATT_WIDTH + 4 * CONV_WIDTH
CONV_K = 3
DILATED_CONFIGS = ((128, 1), (512, 4), (2048, 16))
NUM_BUCKETS = 32
MAX_DISTANCE = 1024
Q_BLOCK = 128


def rms_norm_3(x, g):
    xf = x.astype(jnp.float32)
    y = xf * lax.rsqrt(jnp.mean(xf * xf, axis=-1, keepdims=True) + EPS)
    return (y * g.astype(jnp.float32)).astype(x.dtype)

def dilated_offsets(window, dilation):
    half = window // (2 * dilation)
    return jnp.arange(-half, half + 1, dtype=jnp.int32) * dilation

def t5_bucket(rel):
    nb = NUM_BUCKETS // 2
    max_exact = nb // 2
    ret = jnp.where(rel > 0, nb, 0)
    n = jnp.abs(rel)
    nf = jnp.maximum(n, 1).astype(jnp.float32)
    large = max_exact + (jnp.log(nf / max_exact) / math.log(MAX_DISTANCE / max_exact)
                         * (nb - max_exact)).astype(jnp.int32)
    large = jnp.minimum(large, nb - 1)
    return ret + jnp.where(n < max_exact, n, large)

def dilated_attention(q, k, v, rel_bias):
    B, S, H, hd = q.shape
    qf = (q.astype(jnp.float32) * (hd ** -0.5)).transpose(0, 2, 1, 3)
    kf = k.astype(jnp.float32).transpose(0, 2, 1, 3)
    vf = v.astype(jnp.float32).transpose(0, 2, 1, 3)
    offsets = [dilated_offsets(w, d) for (w, d) in DILATED_CONFIGS]
    biases = [rel_bias.astype(jnp.float32)[t5_bucket(o)].T for o in offsets]

    def block(n):
        start = n * Q_BLOCK
        qb = lax.dynamic_slice_in_dim(qf, start, Q_BLOCK, axis=2)
        pos = start + jnp.arange(Q_BLOCK, dtype=jnp.int32)
        lses, outs = [], []
        for off, bias in zip(offsets, biases):
            idx = pos[:, None] + off[None, :]
            valid = (idx >= 0) & (idx < S)
            idx = jnp.clip(idx, 0, S - 1)
            kg = jnp.take(kf, idx, axis=2)
            vg = jnp.take(vf, idx, axis=2)
            s = jnp.einsum('bhqd,bhqmd->bhqm', qb, kg) + bias[None, :, None, :]
            s = jnp.where(valid[None, None], s, -jnp.inf)
            lse = jax.nn.logsumexp(s, axis=-1)
            p = jnp.exp(s - lse[..., None])
            outs.append(jnp.einsum('bhqm,bhqmd->bhqd', p, vg))
            lses.append(lse)
        w = jax.nn.softmax(jnp.stack(lses, axis=0), axis=0)
        return jnp.sum(w[..., None] * jnp.stack(outs, axis=0), axis=0)

    o = lax.map(block, jnp.arange(S // Q_BLOCK, dtype=jnp.int32))
    return o.transpose(1, 0, 3, 2, 4).reshape(B, S, H * hd)

def short_conv(z, w):
    zp = jnp.pad(z, ((0, 0), (1, 1), (0, 0)))
    return zp[:, :-2] * w[0] + zp[:, 1:-1] * w[1] + zp[:, 2:] * w[2]

def third_inputs(seed: int = 0) -> dict:
    key = jax.random.key(seed)
    ks = jax.random.split(key, 10)
    f32 = jnp.float32
    x = jax.random.normal(ks[0], (BATCH, SEQ, D_MODEL), f32)
    c = jax.random.normal(ks[1], (BATCH, D_MODEL), f32)
    w_ada = jax.random.normal(ks[2], (DEPTH_3, D_MODEL, 3 * D_MODEL), f32) * (0.5 * D_MODEL ** -0.5)
    b_ada = jax.random.normal(ks[3], (DEPTH_3, 3 * D_MODEL), f32) * 0.02
    pre_norm_g = 1.0 + 0.05 * jax.random.normal(ks[4], (DEPTH_3, D_MODEL), f32)
    w_in = jax.random.normal(ks[5], (DEPTH_3, D_MODEL, IN_COLS), f32) * (D_MODEL ** -0.5)
    conv_w = jax.random.normal(ks[6], (DEPTH_3, CONV_K, CONV_WIDTH), f32) * (CONV_K ** -0.5)
    rel_bias = jax.random.normal(ks[7], (NUM_BUCKETS, N_ATT_HEADS), f32) * 0.5
    w_out = jax.random.normal(ks[8], (DEPTH_3, MIX_WIDTH, D_MODEL), f32) * (MIX_WIDTH ** -0.5)
    post_norm_g = 1.0 + 0.05 * jax.random.normal(ks[9], (DEPTH_3, D_MODEL), f32)
    return {"x": x, "c": c, "w_ada": w_ada, "b_ada": b_ada, "pre_norm_g": pre_norm_g,
            "w_in": w_in, "conv_w": conv_w, "rel_bias": rel_bias, "w_out": w_out,
            "post_norm_g": post_norm_g}

def third_block(x, c, w_ada, b_ada, pre_norm_g, w_in, conv_w, rel_bias, w_out, post_norm_g):
    B, S, _ = x.shape
    A, Cw = ATT_WIDTH, CONV_WIDTH
    c_act = jax.nn.silu(c)
    for l in range(DEPTH_3):
        mod = c_act @ w_ada[l] + b_ada[l]
        shift, scale, gate = jnp.split(mod, 3, axis=-1)
        h = rms_norm_3(x, pre_norm_g[l]) * (1.0 + scale[:, None, :]) + shift[:, None, :]
        proj = h @ w_in[l]
        q = proj[..., 0:A].reshape(B, S, N_ATT_HEADS, HEAD_DIM)
        k = proj[..., A:2 * A].reshape(B, S, N_ATT_HEADS, HEAD_DIM)
        v = proj[..., 2 * A:3 * A].reshape(B, S, N_ATT_HEADS, HEAD_DIM)
        g_att = proj[..., 3 * A:4 * A]
        o0 = 4 * A
        u = proj[..., o0:o0 + Cw]
        b_gate = proj[..., o0 + Cw:o0 + 2 * Cw]
        c_gate = proj[..., o0 + 2 * Cw:o0 + 3 * Cw]
        g_conv = proj[..., o0 + 3 * Cw:o0 + 4 * Cw]
        att = dilated_attention(q, k, v, rel_bias).astype(h.dtype) * jax.nn.silu(g_att)
        cnv = b_gate * short_conv(c_gate * u, conv_w[l]) * jax.nn.silu(g_conv)
        mix = jnp.concatenate([att, cnv], axis=-1) @ w_out[l]
        x = x + gate[:, None, :] * rms_norm_3(mix, post_norm_g[l])
    return x


def setup_inputs(seed=0):
    out = dict(first_inputs(seed))
    for name, value in second_inputs(seed + 1).items():
        if name != "x":
            out[name + "_2"] = value
    for name, value in third_inputs(seed + 2).items():
        if name != "x":
            out[name + "_3"] = value
    return out


def reference(
    x, c, ctx, c_ctx, w_ada, b_ada, g_mix, w_in, w_fourier, lb_logits, g_rec, w_out, g_ffn,
    w_router, w_exp_gate, w_exp_up, w_exp_down, g_final, c_2, w_ada_2, b_ada_2, g_mix_2, w_in_2,
    w_proj_attn_2, g_sgu_2, w_sgu_2, b_sgu_2, w_proj_sgu_2, w_out_2, g_ffn_2, w_ff1_2, w_ff2_2,
    g_final_2, c_3, w_ada_3, b_ada_3, pre_norm_g_3, w_in_3, conv_w_3, rel_bias_3, w_out_3,
    post_norm_g_3,
):
    x = first_block(
        x, c, ctx, c_ctx, w_ada, b_ada, g_mix, w_in, w_fourier, lb_logits, g_rec, w_out, g_ffn,
        w_router, w_exp_gate, w_exp_up, w_exp_down, g_final,
    )
    x = second_block(
        x, c_2, w_ada_2, b_ada_2, g_mix_2, w_in_2, w_proj_attn_2, g_sgu_2, w_sgu_2, b_sgu_2,
        w_proj_sgu_2, w_out_2, g_ffn_2, w_ff1_2, w_ff2_2, g_final_2,
    )
    return third_block(
        x, c_3, w_ada_3, b_ada_3, pre_norm_g_3, w_in_3, conv_w_3, rel_bias_3, w_out_3,
        post_norm_g_3,
    )


_drawn_inputs = setup_inputs


def setup_inputs(seed=0):
    import zlib

    import numpy as np

    out = dict(_drawn_inputs(seed))
    spreads = {}
    factors = {'ctx': 2.885,
     'c_ctx': 3.389,
     'g_mix': 4.074,
     'lb_logits': 3.625,
     'g_rec': 7.449,
     'g_ffn': 3.747,
     'b_ada_3': 8.0,
     'pre_norm_g_3': 7.95,
     'rel_bias_3': 8.0,
     'post_norm_g_3': 8.0}
    for name, (base, spread) in spreads.items():
        noise = np.random.default_rng([zlib.crc32(name.encode()), seed]).standard_normal(out[name].shape)
        drawn = base * np.exp(spread * noise) if base else spread * noise
        out[name] = jnp.asarray(drawn.astype(out[name].dtype))
    for name, factor in factors.items():
        out[name] = (out[name] * factor).astype(out[name].dtype)
    return out
```

```python
from contextlib import ExitStack

import numpy as np

import concourse.bass as bass
from concourse import mybir

F32 = mybir.dt.float32
I32 = mybir.dt.int32
ALU = mybir.AluOpType
ACT = mybir.ActivationFunctionType
AX_X = mybir.AxisListType.X

P = 128
T = 256
NT = T // P
D = 1024
KD = D // P
EPS = 1e-6
HEADS = 4
EXPERTS = 16
SLOTS = 2 * T // EXPERTS
F_EXP = 2816
CG = 4
FJ = F_EXP // CG
FC = F_EXP // P
ATT = 8
FF = 4096
LAYERS3 = 2
NEG = -1e30

WCOL = 384
UNIT = KD * WCOL
RING = 6
ADA_PASS = 3072
ADA_J = ADA_PASS // CG
EXP_UNITS = 24
LEVELS = 8

VECTORS = [("c", 8), ("c_ctx", 8), ("c_2", 8), ("c_3", 8), ("b_ada", 48), ("g_mix", 8), ("lb_logits", 16),
           ("g_rec", 4), ("g_ffn", 8), ("g_final", 8), ("b_ada_2", 48), ("g_mix_2", 8), ("g_ffn_2", 8),
           ("g_final_2", 8), ("b_ada_3", 48), ("pre_norm_g_3", 16), ("post_norm_g_3", 16), ("conv_w_3", 24)]
VCOL = {}
_at = 0
for _n, _k in VECTORS:
    VCOL[_n] = _at
    _at += _k
NVEC = _at

CONSTS = [("ident", 128), ("ones", 128), ("dft_feat", 256), ("dft_cos", 512), ("dft_sin", 512),
          ("causal", 512), ("tri", 128), ("slots", 32), ("levels", LEVELS * 128)]
CCOL = {}
_at = 0
for _n, _k in CONSTS:
    CCOL[_n] = (_at, _k)
    _at += _k
NCONST = _at


def constants():
    out = np.zeros((P, NCONST), np.float32)

    def put(name, a):
        at, k = CCOL[name]
        out[:, at:at + k] = np.asarray(a).reshape(P, k)

    i = np.arange(P)
    t = np.arange(T)
    put("ident", np.eye(P))
    put("ones", np.ones((P, P)))
    ang = 2 * np.pi * (np.outer(i, i) % P) / P
    put("dft_feat", np.concatenate([np.cos(ang), np.sin(ang)], 1))
    ang = 2 * np.pi * (np.outer(t, t) % T) / T
    norm = 1 / np.sqrt(T * P)
    put("dft_cos", (np.cos(ang) * norm).reshape(NT, P, T).transpose(1, 0, 2))
    put("dft_sin", (-np.sin(ang) * norm).reshape(NT, P, T).transpose(1, 0, 2))
    put("causal", np.where(t[None, :] <= t[:, None], 0.0, NEG).reshape(NT, P, T).transpose(1, 0, 2))
    put("tri", (i[:, None] <= i[None, :]).astype(np.float32))
    put("slots", np.broadcast_to(np.arange(1, SLOTS + 1), (P, SLOTS)))
    lv = np.zeros((P, LEVELS, P))
    for n in range(LEVELS - 1):
        m = 1 << n
        a, b = i[:, None], i[None, :]
        lv[:, n] = (a // (2 * m) == b // (2 * m)) & (a // m != b // m)
    lv[:, LEVELS - 1] = np.eye(P)
    put("levels", lv)
    off = np.arange(-(T - 1), T)
    n = np.abs(off)
    large = 8 + (np.log(np.maximum(n, 1).astype(np.float32) / np.float32(8)) / np.float32(np.log(128.0))
                 * np.float32(8)).astype(np.int32)
    bucket = np.where(off > 0, 16, 0) + np.where(n < 8, n, np.minimum(large, 15))
    count = sum(((n <= w // 2) & (n % d == 0)).astype(int) for w, d in ((128, 1), (512, 4), (2048, 16)))
    offsets = np.zeros((33, 512), np.float32)
    offsets[bucket, np.arange(off.size)] = 1.0
    offsets[32, :off.size] = np.where(count > 0, np.log(np.maximum(count, 1)), NEG)
    return out, offsets


class Plan:

    def __init__(self):
        self.n = 0
        self.ready = {}
        self.fill = [0] * RING
        self.blocks = 0
        self.inner = 0

    def unit(self, dmas=1):
        u = self.n
        self.n += 1
        self.fill[u % RING] += 16 * dmas
        self.ready[u] = self.fill[u % RING]
        return u

    def block(self, u, last, **kw):
        b = self.blocks
        self.blocks += 1
        if last:
            done = ("unit_used", u + 1)
        else:
            self.inner += 1
            done = ("block_done", self.inner)
        return dict(u=u, b=b, last=last, done=done, **kw)

    def dense(self, cols, kinds):
        units = []
        for c0 in range(0, cols, WCOL):
            w = min(WCOL, cols - c0)
            u = self.unit()
            todo = [(n, k) for n in range(c0 // P, (c0 + w) // P) for k in kinds(n)]
            items = [self.block(u, i == len(todo) - 1, n=n, kind=k, col=n * P - c0)
                     for i, (n, k) in enumerate(todo)]
            units.append(dict(u=u, c0=c0, w=w, items=items))
        return units


def build(nc, inp, scratch, out):
    plan = Plan()
    ada = [[plan.unit() for _ in range(KD)]]

    def in1_kinds(n):
        lat = "T" if 8 <= n < 12 else "F"
        return [(lat, "lat")] + ([(lat, "ctx")] if 8 <= n < 20 else [])

    in1 = plan.dense(3072, in1_kinds)
    ada += [[plan.unit() for _ in range(KD)] for _ in range(3)]
    out1 = plan.dense(D, lambda n: [("F", "cat")])
    ada += [[plan.unit() for _ in range(KD)] for _ in range(2)]
    exp0 = plan.n
    for _ in range(EXPERTS * EXP_UNITS):
        plan.unit()
    assert EXP_UNITS % RING == 0
    in2 = plan.dense(4608, lambda n: [("T" if 8 <= n < 12 or 16 <= n < 20 else "F", "lat")])
    proj2 = []
    for c0 in range(0, D, WCOL):
        w = min(WCOL, D - c0)
        u = plan.unit(2)
        ns = range(c0 // P, (c0 + w) // P)
        proj2.append(dict(u=u, c0=c0, w=w, items=[
            plan.block(u, n == ns[-1] and s == 1, n=n, col=n * P - c0, src=s) for n in ns for s in (0, 1)]))
    out2 = plan.dense(D, lambda n: [("F", "merged")])
    ff1 = plan.dense(FF, lambda n: [("F", "lat")])
    ff2 = []
    for c0 in range(0, D, WCOL):
        w = min(WCOL, D - c0)
        us = [plan.unit() for _ in range(FF // D)]
        ns = range(c0 // P, (c0 + w) // P)
        ff2.append(dict(us=us, c0=c0, w=w, items=[plan.block(us[-1], n == ns[-1], n=n, col=n * P - c0) for n in ns]))
    in3, out3 = [], []
    for _ in range(LAYERS3):
        in3.append(plan.dense(FF, lambda n: [("T" if 8 <= n < 12 else "F", "lat")]))
        out3.append(plan.dense(D, lambda n: [("F", "cat")]))
    total_units = plan.n

    ctx = ExitStack()
    with ctx:
        sems = {}

        def S(name):
            if name not in sems:
                sems[name] = ctx.enter_context(nc.semaphore(name))
            return sems[name]

        w_ready = [S(f"w_ready{i}") for i in range(RING)]

        def sb(name, shape, dt=F32):
            return ctx.enter_context(nc.sbuf_tensor(name, shape, dt))[:]

        ring = sb("ring", [P, RING, UNIT])
        X = sb("X", [P, KD, T])
        vec = sb("vec", [P, NVEC])
        const = sb("const", [P, NCONST])
        conds = sb("conds", [P, KD, 32])
        rows = sb("rows", [P, 2, ADA_J // 2])
        mod = sb("mod", [P, 6, 24])
        modc = sb("modc", [P, 24])
        scl = sb("scl", [P, 8, 8])
        rs = sb("rs", [P, HEADS * T])
        small = sb("small", [P, 64])
        WR = sb("WR", [P, KD, EXPERTS])
        arena = sb("arena", [P, 26 * 1024])
        ps = ctx.enter_context(nc.psum_tensor("ps", [P, 8, 512], F32))

        def ar(at, *shape):
            n = 1
            for s in shape:
                n *= s
            a = arena[:, at:at + n]
            if len(shape) == 2:
                a = a.rearrange("p (a b) -> p a b", a=shape[0])
            if len(shape) == 3:
                a = a.rearrange("p (a b c) -> p a b c", a=shape[0], b=shape[1])
            return a

        def C(name):
            at, k = CCOL[name]
            return const[:, at:at + k]

        ident, ones = C("ident"), C("ones")

        def V(name, n=0, k=1):
            return vec[:, VCOL[name] + n:VCOL[name] + n + k]

        K1 = 1024
        SQ = ar(0, KD, T)
        XN = ar(2 * K1, KD, T)
        H = ar(4 * K1, KD, T)
        CTX = ar(6 * K1, KD, T)
        HC = ar(8 * K1, KD, T)
        FG = ar(10 * K1, 8, T)
        KG = ar(12 * K1, 8, T)
        FGC = ar(14 * K1, 8, T)
        KGC = ar(16 * K1, 8, T)
        U = ar(18 * K1, HEADS, T)
        Q = ar(19 * K1, HEADS, T)
        VT = ar(20 * K1, NT, 512)
        VC = ar(21 * K1, NT, 512)
        SG = ar(22 * K1, HEADS, T)
        TA = ar(23 * K1, 1024)
        TB = ar(24 * K1, 512)
        TAC = ar(8 * K1, 1024)
        TBC = ar(9 * K1, 512)
        DFT = ar(2 * K1, NT, HEADS, T)
        QG = ar(0, 8, T)
        AT = ar(6 * K1, NT, HEADS, T)
        KT = ar(8 * K1, NT, 8, P)
        S0 = ar(14 * K1, 8, P)
        CAT = ar(4 * K1, KD, T)
        Z = ar(18 * K1, HEADS, T)
        WF = ar(24 * K1 + 512, HEADS, P)
        HTOK = ar(6 * K1, NT, D)
        XS = ar(8 * K1, KD, EXPERTS * SLOTS)
        PG = ar(0, NT, EXPERTS, SLOTS)
        SEL = ar(1 * K1, NT, EXPERTS, SLOTS)
        PGT = ar(12 * K1, EXPERTS, T)
        SIL = ar(16 * K1, 2, FJ // 2)
        HID = ar(17 * K1, FJ)
        HIDT = ar(18 * K1, FC, SLOTS)
        YE = ar(19 * K1, 256)
        XCUR = ar(19 * K1 + 256, KD, SLOTS)
        PGCUR = ar(19 * K1 + 512, T)
        PG4 = [ar(20 * K1 + 256 * i, NT, CG * SLOTS) for i in range(2)]
        MOE = ar(2 * K1, KD, T)
        AFFT = ar(21 * K1, T)
        WORK = ar(21 * K1 + 256, T)
        MASK = ar(21 * K1 + 512, T)
        POS = ar(21 * K1 + 768, T)
        AFF = ar(22 * K1, NT, EXPERTS)
        POST = ar(22 * K1 + 32, NT, EXPERTS)
        ONE = ar(22 * K1 + 256, T)
        RELB = ar(23 * K1, ATT, P)
        OFFS = ar(24 * K1, 512)
        REL = ar(24 * K1 + 512, ATT)
        BROW = ar(25 * K1, 2, 512)
        QA = ar(6 * K1, 4, T)
        KA = ar(7 * K1, 4, T)
        VA = ar(8 * K1, NT, 512)
        UA = ar(9 * K1, 4, T)
        VS = ar(10 * K1, NT, 512)
        GA = ar(11 * K1, KD, T)
        GB = ar(13 * K1, KD, T)
        SC = ar(15 * K1, 2, 512)
        PT = ar(16 * K1, 2, 512)
        AO = ar(17 * K1, 4, T)
        SGO = ar(18 * K1, 4, T)
        VSN = ar(19 * K1, NT, 512)
        WS = ar(20 * K1, ATT, P)
        GS = ar(21 * K1, 512)
        BS = ar(21 * K1 + 512, 4, P)
        MG = H
        HFF = ar(8 * K1, FF // P, T)
        HQ = ar(9 * K1, 4, T)
        CU = ar(10 * K1, 4, T)
        CB = ar(11 * K1, 4, T)
        CC = ar(12 * K1, 4, T)
        CS = ar(13 * K1, 4, T)
        ZP = ar(22 * K1, 4, T + 2)
        BIAS = ar(18 * K1, ATT, NT * T)
        MIX3 = ar(15 * K1, KD, T)
        CAT3 = ar(24 * K1, KD, T)

        def slot(u, *shape):
            n = 1
            for s in shape:
                n *= s
            a = ring[:, u % RING, 0:n]
            if len(shape) == 2:
                return a.rearrange("p (a b) -> p a b", a=shape[0])
            if len(shape) == 3:
                return a.rearrange("p (a b c) -> p a b c", a=shape[0], b=shape[1])
            return a

        block = ctx.enter_context(nc.Block())
        SMALL_LOADS = 3

        @block.sync
        def _(sp):
            def load(u, dst, src):
                if u >= RING:
                    sp.wait_ge(S("unit_used"), u - RING + 1)
                sp.dma_start(dst, src).then_inc(w_ready[u % RING], 16)

            def load_ada(p):
                w, h = [(inp["w_ada"][0], 0), (inp["w_ada"][0], 1), (inp["w_ada_2"][0], 0),
                        (inp["w_ada_2"][0], 1), (inp["w_ada_3"][0], 0), (inp["w_ada_3"][1], 0)][p]
                for kc, u in enumerate(ada[p]):
                    load(u, slot(u, ADA_PASS), w[kc * P:(kc + 1) * P, h * ADA_PASS:(h + 1) * ADA_PASS])

            def load_dense(units, w):
                view = w.rearrange("(k p) n -> p k n", p=P)
                for g in units:
                    load(g["u"], slot(g["u"], KD, g["w"]), view[:, :, g["c0"]:g["c0"] + g["w"]])

            load_ada(0)
            load_dense(in1, inp["w_in"][0])
            for p in (1, 2, 3):
                load_ada(p)
            load_dense(out1, inp["w_out"][0])
            for p in (4, 5):
                load_ada(p)

            gate = inp["w_exp_gate"].rearrange("a e (k p) f -> (a e) p k f", p=P)
            up = inp["w_exp_up"].rearrange("a e (k p) f -> (a e) p k f", p=P)
            down = inp["w_exp_down"].rearrange("a e (p c) d -> (a e) p (c d)", p=P)
            with sp.Fori(0, EXPERTS) as e:
                for k in range(EXP_UNITS):
                    sp.wait_ge(S("unit_used"), e * EXP_UNITS + (exp0 + k - RING + 1))
                    s = (exp0 + k) % RING
                    if k < 16:
                        src = (gate if k < 8 else up)[e, :, k % 8, :]
                        dst = ring[:, s, 0:F_EXP]
                    else:
                        c0 = 3 * (k - 16)
                        c1 = min(c0 + 3, FC)
                        src = down[e, :, c0 * D:c1 * D]
                        dst = ring[:, s, 0:(c1 - c0) * D]
                    sp.dma_start(dst, src).then_inc(w_ready[s], 16)

            load_dense(in2, inp["w_in_2"][0])
            pa = inp["w_proj_attn_2"][0].rearrange("(k p) n -> p k n", p=P)
            pb = inp["w_proj_sgu_2"][0].rearrange("(k p) n -> p k n", p=P)
            for g in proj2:
                dst = slot(g["u"], 2, 4, g["w"])
                load(g["u"], dst[:, 0], pa[:, :, g["c0"]:g["c0"] + g["w"]])
                load(g["u"], dst[:, 1], pb[:, :, g["c0"]:g["c0"] + g["w"]])
            load_dense(out2, inp["w_out_2"][0])
            load_dense(ff1, inp["w_ff1_2"][0])
            v = inp["w_ff2_2"][0].rearrange("(b k p) n -> b p k n", b=FF // D, p=P)
            for g in ff2:
                for b, u in enumerate(g["us"]):
                    load(u, slot(u, KD, g["w"]), v[b, :, :, g["c0"]:g["c0"] + g["w"]])
            for l in range(LAYERS3):
                load_dense(in3[l], inp["w_in_3"][l])
                load_dense(out3[l], inp["w_out_3"][l])
            sp.wait_ge(S("x_final"), 1)
            sp.dma_start(out, X[:]).then_inc(S("stored"), 16)
            sp.wait_ge(S("stored"), 16)

        @block.tensor
        def _(pe):
            def unit_ready(u):
                pe.wait_ge(w_ready[u % RING], plan.ready[u])

            def count(ins, name):
                ins.then_inc(S(name), 1)

            def ada_unit(p, kc):
                u = ada[p][kc]
                unit_ready(u)
                if kc == 0 and p > 0:
                    pe.wait_ge(S("rows_out"), p)
                for i in range(2):
                    for j in range(CG):
                        at = ADA_J * j + ADA_J // 2 * i
                        m = pe.matmul(ps[32 * j:32 * j + 32, 6 + i, 0:ADA_J // 2], conds[:, kc, :],
                                      ring[:, u % RING, at:at + ADA_J // 2], start=(kc == 0),
                                      stop=(kc == KD - 1), skip_group_check=True)
                count(m, "unit_used")

            def turn(p):
                pe.wait_ge(S("rows_out"), p + 1)
                if p > 0:
                    pe.wait_ge(S("mod_ready"), p)
                pick = ident.rearrange("p (j c) -> p j c", j=CG)[:, :, 0:4]
                for q in range(6):
                    m = pe.matmul(ps[:, 4, 16 * q:16 * q + 16], rows[:, q // 3, P * (q % 3):P * (q % 3) + P], pick,
                                  start=True, stop=True, skip_group_check=True)
                count(m, "turned")

            def dense(units, src, K=KD, bank0=0):
                for g in units:
                    unit_ready(g["u"])
                    w = slot(g["u"], K, g["w"])
                    for it in g["items"]:
                        if it["b"] >= 4:
                            pe.wait_ge(S("evacuated"), it["b"] - 3)
                        bank = it["b"] % 4
                        h = src(it)
                        for t in range(NT if it["kind"][0] == "T" else 1):
                            for k in range(K):
                                wk = w[:, k, it["col"]:it["col"] + P]
                                if it["kind"][0] == "T":
                                    m = pe.matmul(ps[:, bank, P * t:P * t + P], h[:, k, P * t:P * t + P], wk,
                                                  start=(k == 0), stop=(k == K - 1))
                                else:
                                    m = pe.matmul(ps[:, bank, 0:T], wk, h[:, k, :], start=(k == 0),
                                                  stop=(k == K - 1))
                        count(m, "unit_used" if it["last"] else "block_done")

            norms = [0]

            def sum_squares(sq=SQ):
                norms[0] += 1
                pe.wait_ge(S("squared"), norms[0])
                for c in range(KD):
                    m = pe.matmul(ps[:, 5, 0:T], ones, sq[:, c, :], start=(c == 0), stop=(c == KD - 1))
                count(m, "summed")

            modulated = [0]

            def wait_h():
                modulated[0] += KD
                pe.wait_ge(S("modulated"), modulated[0])

            pe.wait_ge(S("small_in"), 16 * SMALL_LOADS)
            pe.wait_ge(S("conds_ready"), 1)
            for kc in range(KD):
                ada_unit(0, kc)
            turn(0)
            sum_squares()
            sum_squares()
            wait_h()
            wait_h()
            dense(in1, lambda it: H if it["kind"][1] == "lat" else HC)

            pe.wait_ge(S("evacuated"), in1[-1]["items"][-1]["b"] + 1)
            todo = [(1, k) for k in range(KD)] + [(2, k) for k in range(KD)] + [(3, k) for k in range(KD)]

            def fill(k):
                for _ in range(k):
                    if todo:
                        p, kc = todo.pop(0)
                        ada_unit(p, kc)
                        if kc == KD - 1:
                            turn(p)

            for t in range(NT):
                for g in range(HEADS):
                    m = pe.matmul(ps[:, 2 * t + g // 2, T * (g % 2):T * (g % 2) + T], U[:, g, P * t:P * t + P],
                                  C("dft_feat"), start=True, stop=True)
            count(m, "dft_feat")
            fill(2)
            pe.wait_ge(S("dft_out"), 1)
            for g in range(HEADS):
                for i, w in enumerate(("dft_cos", "dft_sin")):
                    for t in range(NT):
                        m = pe.matmul(ps[:, g, 0:T], DFT[:, t, g, P * i:P * i + P], C(w)[:, T * t:T * t + T],
                                      start=(i == 0 and t == 0), stop=(i == 1 and t == 1))
            count(m, "dft_tok")
            pe.wait_ge(S("z_out"), 1)
            for g in range(HEADS):
                m = pe.matmul(ps[:, g, 0:T], WF[:, g, :], Z[:, g, :], start=True, stop=True)
            count(m, "fourier")
            fill(1)

            pe.wait_ge(S("kg_ready"), 1)
            pe.wait_ge(S("fourier_out"), 1)
            for t in range(NT):
                for h in range(HEADS):
                    for d in range(2):
                        m = pe.matmul(ps[:, t, P * h:P * h + P], KG[:, 4 * d + h, P * t:P * t + P],
                                      Q[:, h, P * t:P * t + P], start=(d == 0), stop=(d == 1))
            count(m, "level")
            for n in range(LEVELS):
                if n >= 1:
                    pe.wait_ge(S("qk_ready"), n)
                    pe.wait_ge(S("level_out"), n)
                base = 2 * ((n + 1) % 2)
                if n < LEVELS - 1:
                    mm = 1 << n
                    for t in range(NT):
                        for h in range(HEADS):
                            for d in range(2):
                                half = 1 - d
                                o = ps[:, base + t, P * h:P * h + P].rearrange("p (b two m) -> p b two m", two=2, m=mm)
                                r = QG[:, 4 * d + h, P * t:P * t + P].rearrange("p (b two m) -> p b two m", two=2, m=mm)
                                m = pe.matmul(o[:, :, half, :], KG[:, 4 * d + h, P * t:P * t + P],
                                              r[:, :, half, :], start=True, stop=True, skip_group_check=True)
                else:
                    for h in range(HEADS):
                        for d in range(2):
                            m = pe.matmul(ps[:, base + d, P * h:P * h + P], KG[:, 4 * d + h, P * d:P * d + P],
                                          QG[:, 4 * d + h, P * (1 - d):P * (1 - d) + P], start=True, stop=True,
                                          skip_group_check=True)
                count(m, "level")
                fill(3 if n < LEVELS - 1 else 0)

            pe.wait_ge(S("kgc_ready"), 1)
            pe.wait_ge(S("level_out"), LEVELS + 1)
            for t in range(NT):
                for g in range(8):
                    m = pe.transpose(ps[:, 2 * t + g // 4, P * (g % 4):P * (g % 4) + P], KGC[:, g, P * t:P * t + P], ident)
            count(m, "kt")
            pe.wait_ge(S("kt_out"), 4)
            for g in range(8):
                for t in range(NT):
                    m = pe.matmul(ps[:, g // 4, P * (g % 4):P * (g % 4) + P], KT[:, t, g, :],
                                  VC[:, t, P * (g % 4):P * (g % 4) + P], start=(t == 0), stop=(t == 1))
            count(m, "s0")
            pe.wait_ge(S("s0_out"), 2)
            for h in range(HEADS):
                for t in range(NT):
                    pe.matmul(ps[:, h, 0:T], VT[:, t, P * h:P * h + P], AT[:, t, h, :], start=(t == 0), stop=False)
                for d in range(2):
                    m = pe.matmul(ps[:, h, 0:T], S0[:, 4 * d + h, :], QG[:, 4 * d + h, :], start=False, stop=(d == 1))
            count(m, "o_done")
            pe.wait_ge(S("o_squared"), 1)
            for i in range(2):
                m = pe.matmul(ps[:, 4 + i, :], ones, SQ[:, 2 * i:2 * i + 2, :], start=True, stop=True)
            count(m, "o_summed")
            pe.wait_ge(S("rec_ready"), 1)
            dense(out1, lambda it: CAT)

            todo += [(4, k) for k in range(KD)] + [(5, k) for k in range(KD)]
            fill(3)
            sum_squares()
            fill(2)
            wait_h()
            pe.wait_ge(S("evacuated"), out1[-1]["items"][-1]["b"] + 1)
            for t in range(NT):
                for k in range(KD):
                    m = pe.matmul(ps[:, 5, 16 * t:16 * t + 16], H[:, k, P * t:P * t + P], WR[:, k, :],
                                  start=(k == 0), stop=(k == KD - 1))
            count(m, "logits")
            for t in range(NT):
                for k in range(KD):
                    m = pe.transpose(ps[:, 2 * t + k // 4, P * (k % 4):P * (k % 4) + P], H[:, k, P * t:P * t + P], ident)
            count(m, "h_turned")
            fill(3)
            pe.wait_ge(S("aff"), 1)
            for t in range(NT):
                m = pe.transpose(ps[0:16, 5, P * t:P * t + P], AFF[:, t, :], ident)
            count(m, "aff_turned")
            fill(4)
            pe.wait_ge(S("pos"), 1)
            for t in range(NT):
                m = pe.transpose(ps[:, 5, 16 * t:16 * t + 16], POS[0:16, P * t:P * t + P], ident[0:16, 0:16])
            count(m, "pos_turned")
            fill(16)
            pe.wait_ge(S("sel"), 1)
            pe.wait_ge(S("h_tok"), 4)
            for c in range(KD):
                if c >= 4:
                    pe.wait_ge(S("xs_out"), c - 3)
                for t in range(NT):
                    m = pe.matmul(ps[:, c % 4, :], HTOK[:, t, P * c:P * c + P], SEL[:, t, :, :],
                                  start=(t == 0), stop=(t == NT - 1))
                count(m, "xs")
            pe.wait_ge(S("mod_ready"), 6)
            for e in range(EXPERTS):
                pe.wait_ge(S("pg4"), e + 1)
                if e >= 2:
                    pe.wait_ge(S("pgt_out"), e - 1)
                for t in range(NT):
                    m = pe.transpose(ps[:, 4 + e % 2, P * t:P * t + P],
                                     PG4[e % 2][:, t, :], ident)
                count(m, "pgt")
            pe.wait_ge(S("relb"), 1)
            pe.wait_ge(S("xs_out"), KD)
            for h in range(ATT):
                if h >= 2:
                    pe.wait_ge(S("brow_out"), h - 1)
                m = pe.matmul(ps[:, h % 2, 0:511], RELB[0:33, h, :], OFFS[0:33, 0:511], start=True, stop=True)
                count(m, "brow")
            pe.wait_ge(S("brow_out"), ATT)
            pe.wait_ge(S("pgt_out"), EXPERTS)

            pe.sem_inc(S("scattered"), 1)
            with pe.Fori(0, EXPERTS) as e:
                pe.wait_ge(S("xcur"), e + 1)
                pe.wait_ge(S("hid_done"), e + 1)
                for k in range(16):
                    s = (exp0 + k) % RING
                    pe.wait_ge(w_ready[s], e * (16 * EXP_UNITS // RING) + plan.ready[exp0 + k])
                    for i in range(2):
                        for j in range(CG):
                            at = FJ * j + FJ // 2 * i
                            m = pe.matmul(ps[32 * j:32 * j + 32, 2 * (k // 8) + i, 0:FJ // 2], XCUR[:, k % 8, :],
                                          ring[:, s, at:at + FJ // 2], start=(k % 8 == 0), stop=(k % 8 == 7),
                                          skip_group_check=True)
                    count(m, "unit_used")
                pe.wait_ge(S("hid_t"), e + 1)
                pe.wait_ge(S("acc_done"), e + 1)
                for k in range(16, EXP_UNITS):
                    s = (exp0 + k) % RING
                    pe.wait_ge(w_ready[s], e * (16 * EXP_UNITS // RING) + plan.ready[exp0 + k])
                    c0 = 3 * (k - 16)
                    for c in range(c0, min(c0 + 3, FC)):
                        for j in range(CG):
                            at = D * (c - c0) + T * j
                            m = pe.matmul(ps[32 * j:32 * j + 32, 4, 0:T], HIDT[:, c, :], ring[:, s, at:at + T],
                                          start=(c == 0), stop=(c == FC - 1), skip_group_check=True)
                    count(m, "unit_used")
                pe.wait_ge(S("ye"), e + 1)
                pe.wait_ge(S("pgcur"), e + 1)
                for i in range(2):
                    for j in range(CG):
                        m = pe.matmul(ps[:, 4 + j, T * i:T * i + T], YE[32 * j:32 * j + 32, P * i:P * i + P],
                                      PGCUR[32 * j:32 * j + 32, :], start=True, stop=True)
                count(m, "scattered")

            sum_squares()
            sum_squares()
            wait_h()
            dense(in2, lambda it: H)

            heads_done = [0]

            def attention():
                def scores(h):
                    n = heads_done[0] + h
                    if n >= 2:
                        pe.wait_ge(S("scores_read"), n - 1)
                    r = 64 * (h % 2)
                    for t in range(NT):
                        m = pe.matmul(ps[:, 4 + n % 2, T * t:T * t + T], QA[r:r + 64, h // 2, P * t:P * t + P],
                                      KA[r:r + 64, h // 2, :], start=True, stop=True)
                    count(m, "scores")

                def values(h):
                    n = heads_done[0] + h
                    pe.wait_ge(S("probs"), n + 1)
                    if n >= 1:
                        pe.wait_ge(S("pt_out"), n)
                    for kt in range(NT):
                        for t in range(NT):
                            m = pe.transpose(ps[:, 6, T * kt + P * t:T * kt + P * t + P],
                                             SC[:, n % 2, T * t + P * kt:T * t + P * kt + P], ident)
                    count(m, "pt")
                    pe.wait_ge(S("pt_out"), n + 1)
                    if n >= 2 and h % 2 == 0:
                        pe.wait_ge(S("ao_out"), n // 2)
                    r = 64 * (h % 2)
                    for kt in range(NT):
                        m = pe.matmul(ps[r:r + 64, 7, 0:T], VA[:, kt, 64 * h:64 * h + 64],
                                      PT[:, n % 2, T * kt:T * kt + T], start=(kt == 0), stop=(kt == 1))
                    count(m, "ao")

                scores(0)
                for h in range(ATT):
                    if h + 1 < ATT:
                        scores(h + 1)
                    values(h)
                heads_done[0] += ATT

            pe.wait_ge(S("evacuated"), in2[-1]["items"][-1]["b"] + 1)
            attention()
            pe.wait_ge(S("vsn"), 1)
            for t in range(NT):
                for g in range(ATT):
                    r = 64 * (g % 2)
                    m = pe.matmul(ps[r:r + 64, g // 2, P * t:P * t + P], VSN[:, t, 64 * g:64 * g + 64], WS[:, g, :],
                                  start=True, stop=True, skip_group_check=True)
            count(m, "sgu")
            pe.wait_ge(S("sgo"), 1)
            pe.wait_ge(S("ao_out"), heads_done[0] // 2)
            for g in proj2:
                unit_ready(g["u"])
                w = slot(g["u"], 2, 4, g["w"])
                for it in g["items"]:
                    pe.wait_ge(S("evacuated"), it["b"] - 3)
                    for k in range(4):
                        m = pe.matmul(ps[:, it["b"] % 4, 0:T], w[:, it["src"], k, it["col"]:it["col"] + P],
                                      (AO, SGO)[it["src"]][:, k, :], start=(k == 0), stop=(k == 3))
                    count(m, "unit_used" if it["last"] else "block_done")
            pe.wait_ge(S("merged"), 1)
            dense(out2, lambda it: MG)
            sum_squares()
            wait_h()
            dense(ff1, lambda it: H)
            for g in ff2:
                for b, u in enumerate(g["us"]):
                    unit_ready(u)
                    w = slot(u, KD, g["w"])
                    pe.wait_ge(S("ff_squared"), KD * (b + 1))
                    for it in g["items"]:
                        if b == 0:
                            pe.wait_ge(S("evacuated"), it["b"] - 3)
                        for k in range(KD):
                            m = pe.matmul(ps[:, it["b"] % 4, 0:T], w[:, k, it["col"]:it["col"] + P],
                                          HFF[:, KD * b + k, :], start=(b == 0 and k == 0),
                                          stop=(b == FF // D - 1 and k == KD - 1), skip_group_check=True)
                        if b == FF // D - 1 and not it["last"]:
                            count(m, "block_done")
                    count(m, "unit_used")
            sum_squares()
            for l in range(LAYERS3):
                sum_squares()
                wait_h()
                dense(in3[l], lambda it: H)
                pe.wait_ge(S("evacuated"), in3[l][-1]["items"][-1]["b"] + 1)
                attention()
                pe.wait_ge(S("ao_out"), heads_done[0] // 2)
                pe.wait_ge(S("conv"), l + 1)
                dense(out3[l], lambda it: CAT3)
                sum_squares()

        @block.scalar
        def _(act):
            made = {}

            def link(ins, name):
                made[name] = made.get(name, 0) + 1
                ins.then_inc(S(name), 1)
                act.wait_ge(S(name), made[name])

            def mark(ins, name):
                made[name] = made.get(name, 0) + 1
                ins.then_inc(S(name), 1)

            act.dma_start(vec[:], inp["vec"]).then_inc(S("vec_in"), 16)
            act.dma_start(X[:], inp["xT"]).then_inc(S("x_in"), 16)
            act.dma_start(CTX, inp["ctxT"]).then_inc(S("x_in"), 16)
            for dst, src in ((const[:], inp["const"]), (WF, inp["w_fourier"][0].rearrange("g c d -> c g d")),
                             (WR[:], inp["w_router"][0].rearrange("(k p) e -> p k e", p=P))):
                act.dma_start(dst, src).then_inc(S("small_in"), 16)

            def rows_out(p):
                act.wait_ge(S("unit_used"), ada[p][-1] + 1)
                if p > 0:
                    act.wait_ge(S("turned"), p)
                mark(act.activation(rows[:, :, :], ps[:, 6:8, 0:ADA_J // 2], ACT.Copy), "rows_out")

            def evacuate(it, dst, func=ACT.Copy, scale=1.0):
                act.wait_ge(S(it["done"][0]), it["done"][1])
                mark(act.activation(dst, ps[:, it["b"] % 4, 0:T], func, scale=scale), "evacuated")

            norm_no = [0]

            def modulate(dst, shift, cols=None, src=XN):
                norm_no[0] += 1
                act.wait_ge(S("mean_square"), norm_no[0])
                mark(act.activation(rs[:, 0:T], rs[:, 0:T], ACT.Sqrt), "rooted")
                act.wait_ge(S("normed"), norm_no[0])
                a = norm_no[0] % 8 if cols is None else cols
                for c in range(KD):
                    if shift is None:
                        mark(act.activation(dst[:, c, :], XN[:, c, :], ACT.Copy, scale=scl[:, a, c:c + 1]), "scaled")
                    else:
                        mark(act.activation(dst[:, c, :], XN[:, c, :], ACT.Identity, scale=scl[:, a, c:c + 1],
                                            bias=shift[:, c:c + 1]), "modulated")

            act.wait_ge(S("vec_in"), 16)
            act.wait_ge(S("conds_zero"), 1)
            act.activation(conds[:, :, 0:4].rearrange("p k c -> p c k"),
                           vec[:, 0:32].rearrange("p (c k) -> p c k", c=4), ACT.Silu).then_inc(S("conds_ready"), 1)
            act.wait_ge(S("lb_sub"), 1)
            mark(act.activation(small[:, 16:32], small[:, 0:16], ACT.Exp), "lb_exp")
            rows_out(0)
            modulate(H, mod[:, 0, 0:8])
            modulate(HC, modc[:, 0:8])
            for g in in1:
                for it in g["items"]:
                    n, (kind, which) = it["n"], it["kind"]
                    lat = which == "lat"
                    if n < 4:
                        evacuate(it, U[:, n, :])
                    elif n < 8:
                        evacuate(it, Q[:, n - 4, :], ACT.Silu)
                    elif n < 12:
                        evacuate(it, (VT if lat else VC)[:, :, P * (n - 8):P * (n - 8) + P])
                    elif n < 20:
                        evacuate(it, (FG if lat else FGC)[:, n - 12, :], ACT.Sigmoid)
                    else:
                        evacuate(it, SG[:, n - 20, :], ACT.Silu)
            act.wait_ge(S("dft_feat"), 1)
            mark(act.activation(ar(2 * K1, 4, 512), ps[:, 0:4, :], ACT.Copy), "dft_out")
            act.wait_ge(S("dft_tok"), 1)
            mark(act.activation(Z, ps[:, 0:4, 0:T], ACT.Copy), "z_out")
            act.wait_ge(S("fourier"), 1)
            mark(act.activation(CAT[:, 0:HEADS, :], ps[:, 0:4, 0:T], ACT.Copy), "fourier_out")
            for p in (1, 2, 3):
                rows_out(p)
            act.wait_ge(S("kt"), 1)
            for t in range(NT):
                for i in range(2):
                    mark(act.activation(KT[:, t, 4 * i:4 * i + 4, :],
                                        ps[:, 2 * t + i, :].rearrange("p (g d) -> p g d", g=4), ACT.Copy), "kt_out")
            act.wait_ge(S("s0"), 1)
            for i in range(2):
                mark(act.activation(S0[:, 4 * i:4 * i + 4, :], ps[:, i, :].rearrange("p (g d) -> p g d", g=4),
                                    ACT.Copy), "s0_out")
            act.wait_ge(S("o_mean"), 1)
            mark(act.activation(rs[:, :], rs[:, :], ACT.Sqrt), "o_rooted")
            act.dma_start(REL[0:33, :], inp["rel"]).then_inc(S("rel_in"), 16)
            act.dma_start(OFFS[0:33, :], inp["offsets"]).then_inc(S("rel_in"), 16)
            for g in out1:
                for it in g["items"]:
                    evacuate(it, SQ[:, it["n"], :], ACT.Copy, mod[:, 0, 16 + it["n"]:17 + it["n"]])
            modulate(H, mod[:, 1, 0:8])
            act.wait_ge(S("h_turned"), 1)
            for t in range(NT):
                for i in range(2):
                    mark(act.activation(HTOK[:, t, 512 * i:512 * i + 512], ps[:, 2 * t + i, :], ACT.Copy), "h_tok")
            act.wait_ge(S("logit_max"), 1)
            for t in range(NT):
                mark(act.activation(AFF[:, t, :], AFF[:, t, :], ACT.Exp, bias=small[:, 40 + t:41 + t],
                                    accum_out=small[:, 42 + t:43 + t]), "aff_exp")
            rows_out(4)
            rows_out(5)
            for c in range(KD):
                act.wait_ge(S("xs"), c + 1)
                mark(act.activation(XS[:, c, :], ps[:, c % 4, :], ACT.Copy), "xs_out")
            for e in range(EXPERTS):
                act.wait_ge(S("pgt"), e + 1)
                mark(act.activation(PGT[:, e, :], ps[:, 4 + e % 2, 0:T], ACT.Copy), "pgt_out")
            for h in range(ATT):
                act.wait_ge(S("brow"), h + 1)
                if h >= 2:
                    act.wait_ge(S(f"bias_stored{h % 2}"), 16 * (h // 2))
                link(act.activation(BROW[:, h % 2, 0:511], ps[:, h % 2, 0:511], ACT.Copy), "brow_out")
                act.dma_start(scratch[h:h + 1, 0:P * 512].rearrange("a (q j) -> q (a j)", q=P)[:, 0:511],
                              BROW[:, h % 2, 0:511]).then_inc(S(f"bias_stored{h % 2}"), 16)
            act.wait_ge(S("sel"), 1)
            act.dma_start(WS, inp["w_sgu"]).then_inc(S("sgu_in"), 16)
            act.dma_start(GS, inp["g_sgu"]).then_inc(S("sgu_in"), 16)
            act.dma_start(BS, inp["b_sgu"]).then_inc(S("sgu_in"), 16)

            with act.Fori(0, EXPERTS) as e:
                act.wait_ge(S("unit_used"), e * EXP_UNITS + (exp0 + 8))
                act.wait_ge(S("hid_done"), e + 1)
                act.activation(SIL, ps[:, 0:2, 0:FJ // 2], ACT.Silu).then_inc(S("sil"), 1)
                act.wait_ge(S("unit_used"), e * EXP_UNITS + (exp0 + EXP_UNITS))
                act.wait_ge(S("scattered"), e + 1)
                act.activation(YE, ps[:, 4, 0:T], ACT.Copy).then_inc(S("ye"), 1)

            act.wait_ge(S("acc_done"), EXPERTS + 1)
            for c in range(KD):
                mark(act.activation(SQ[:, c, :], MOE[:, c, :], ACT.Copy, scale=mod[:, 1, 16 + c:17 + c]), "moe_gated")
            modulate(X, None)
            modulate(H, mod[:, 2, 0:8])
            for g in in2:
                for it in g["items"]:
                    n = it["n"]
                    if n < 4:
                        evacuate(it, QA[:, n, :], ACT.Copy, 0.125)
                    elif n < 8:
                        evacuate(it, KA[:, n - 4, :])
                    elif n < 12:
                        evacuate(it, VA[:, :, P * (n - 8):P * (n - 8) + P])
                    elif n < 16:
                        evacuate(it, UA[:, n - 12, :], ACT.Gelu_apprx_tanh)
                    elif n < 20:
                        evacuate(it, VS[:, :, P * (n - 16):P * (n - 16) + P], ACT.Gelu_apprx_tanh)
                    elif n < 28:
                        evacuate(it, GA[:, n - 20, :], ACT.Sigmoid)
                    else:
                        evacuate(it, GB[:, n - 28, :], ACT.Sigmoid)
            act.wait_ge(S("evacuated"), made["evacuated"])
            for t in range(NT):
                link(act.activation(SQ[:, 2 * t:2 * t + 2, :], VS[:, t, :].rearrange("p (a b) -> p a b", a=2),
                                    ACT.Square, accum_out=small[:, 44 + t:45 + t]), "vs_sq")
            act.wait_ge(S("vs_mean"), 1)
            mark(act.activation(small[:, 44:46], small[:, 44:46], ACT.Sqrt), "vs_rooted")

            heads = [0]

            def softmax_exp():
                def exp(n):
                    act.wait_ge(S("row_max"), n + 1)
                    for t in range(NT):
                        mark(act.activation(SC[:, n % 2, T * t:T * t + T], SC[:, n % 2, T * t:T * t + T], ACT.Exp,
                                            bias=small[:, 48 + 2 * (n % 2) + t:49 + 2 * (n % 2) + t],
                                            accum_out=small[:, 52 + 2 * (n % 2) + t:53 + 2 * (n % 2) + t]), "p_exp")

                n0 = heads[0]
                exp(n0)
                for n in range(n0, n0 + ATT):
                    if n + 1 < n0 + ATT:
                        exp(n + 1)
                    act.wait_ge(S("pt"), n + 1)
                    if n >= 2:
                        act.wait_ge(S("ao"), n - 1)
                    mark(act.activation(PT[:, n % 2, :], ps[:, 6, :], ACT.Copy), "pt_out")
                heads[0] += ATT

            softmax_exp()
            for g in proj2:
                for it in g["items"]:
                    evacuate(it, (SQ, XN)[it["src"]][:, it["n"], :])
            for g in out2:
                for it in g["items"]:
                    evacuate(it, SQ[:, it["n"], :], ACT.Copy, mod[:, 2, 16 + it["n"]:17 + it["n"]])
            for i in range(2):
                act.wait_ge(S(f"bias_stored{i}"), 16 * ATT // 2)
            for t in range(NT):
                at = T - 1 - P * t
                view = scratch[:, at:at + P * 511].rearrange("h (q j) -> q h j", j=511)
                act.dma_start(BIAS[:, :, T * t:T * t + T], view[:, :, 0:T]).then_inc(S("bias_in"), 16)
            modulate(H, mod[:, 3, 0:8])
            for g in ff1:
                for it in g["items"]:
                    evacuate(it, HFF[:, it["n"], :], ACT.Relu)
            for g in ff2:
                for it in g["items"]:
                    evacuate(it, SQ[:, it["n"], :], ACT.Copy, mod[:, 3, 16 + it["n"]:17 + it["n"]])
            modulate(X, None)
            for l in range(LAYERS3):
                modulate(H, mod[:, 4 + l, 0:8])
                for g in in3[l]:
                    for it in g["items"]:
                        n = it["n"]
                        if n < 4:
                            evacuate(it, QA[:, n, :], ACT.Copy, 0.125)
                        elif n < 8:
                            evacuate(it, KA[:, n - 4, :])
                        elif n < 12:
                            evacuate(it, VA[:, :, P * (n - 8):P * (n - 8) + P])
                        else:
                            q = (n - 12) // 4
                            evacuate(it, (HQ, CU, CB, CC, CS)[q][:, n % 4, :], ACT.Silu if q in (0, 4) else ACT.Copy)
                softmax_exp()
                for g in out3[l]:
                    for it in g["items"]:
                        evacuate(it, MIX3[:, it["n"], :])
                modulate(SQ, None)

        @block.vector
        def _(dve):
            made = {}

            def link(ins, name="dve_step"):
                made[name] = made.get(name, 0) + 1
                ins.then_inc(S(name), 1)
                dve.wait_ge(S(name), made[name])

            def waits(name, n):
                dve.wait_ge(S(name), n)

            tt, ts, stt = dve.tensor_tensor, dve.tensor_scalar, dve.scalar_tensor_tensor
            norms = [0]

            before = []
            modulations = {"modulated": 0, "scaled": 0}

            def rms(src, gain, plus_one=None, times=None, then="modulated"):
                norms[0] += 1
                k = norms[0]
                if before:
                    waits(*before.pop())
                link(tt(SQ, src, src, ALU.mult), "squared")
                a = scl[:, k % 8, :]
                if times is not None:
                    link(tt(a, gain, times, ALU.mult))
                elif plus_one is None:
                    link(dve.tensor_copy(a, gain))
                else:
                    link(stt(a, plus_one, 1.0, gain, ALU.add, ALU.mult))
                waits("summed", k)
                r = rs[:, 0:T]
                link(ts(r, ps[:, 5, 0:T], 1.0 / D, EPS, ALU.mult, ALU.add), "mean_square")
                waits("rooted", k)
                link(dve.reciprocal(r, r))
                link(tt(XN, src, r.unsqueeze(1).broadcast_to([P, KD, T]), ALU.mult), "normed")
                modulations[then] += KD
                before.append((then, modulations[then]))

            def mod_in(p):
                waits("turned", p + 1)
                bias = [V("b_ada", 0, 24), V("b_ada", 24, 24), V("b_ada_2", 0, 24), V("b_ada_2", 24, 24),
                        V("b_ada_3", 0, 24), V("b_ada_3", 24, 24)][p]
                v = ps[:, 4, 0:96].rearrange("p (q j c) -> p j q c", q=6, j=CG)
                bias = bias.rearrange("p (j q) -> p j q", j=CG)
                if p == 0:
                    link(tt(modc[:, :].rearrange("p (j q) -> p j q", j=CG), v[:, :, :, 1], bias, ALU.add))
                link(tt(mod[:, p, :].rearrange("p (j q) -> p j q", j=CG), v[:, :, :, (0, 0, 2, 2, 3, 3)[p]], bias,
                        ALU.add), "mod_ready")

            def residual(units):
                for g in units:
                    for it in g["items"]:
                        waits("evacuated", it["b"] + 1)
                        link(tt(X[:, it["n"], :], X[:, it["n"], :], SQ[:, it["n"], :], ALU.add))

            link(dve.memset(conds[:], 0.0), "conds_zero")
            waits("vec_in", 16)
            waits("small_in", 16 * SMALL_LOADS)
            lg = V("lb_logits", 0, 16)
            link(tt(small[:, 32:40], lg[:, 0:8], lg[:, 8:16], ALU.max))
            link(tt(small[:, 0:8], lg[:, 0:8], small[:, 32:40], ALU.subtract))
            link(tt(small[:, 8:16], lg[:, 8:16], small[:, 32:40], ALU.subtract), "lb_sub")
            waits("x_in", 32)
            waits("lb_exp", 1)
            link(tt(small[:, 32:40], small[:, 16:24], small[:, 24:32], ALU.add))
            link(dve.reciprocal(small[:, 40:48], small[:, 32:40]))
            link(tt(small[:, 0:8], small[:, 16:24], small[:, 40:48], ALU.mult))
            link(ts(small[:, 8:16], small[:, 0:8], -1.0, 1.0, ALU.mult, ALU.add), "lb_ready")
            mod_in(0)
            rms(X, V("g_mix", 0, 8), mod[:, 0, 8:16])
            rms(CTX, V("g_mix", 0, 8), modc[:, 8:16])

            waits("evacuated", in1[-1]["items"][-1]["b"] + 1)
            link(dve.memset(AT, 0.0))
            for g in range(8):
                link(ts(FG[:, g, :], FG[:, g, :], small[:, 8 + g:9 + g], small[:, g:g + 1], ALU.mult, ALU.add))
            link(ts(KG, FG, -1.0, 1.0, ALU.mult, ALU.add))
            for d in range(2):
                link(tt(QG[:, 4 * d:4 * d + 4, :], Q, FG[:, 4 * d:4 * d + 4, :], ALU.mult),
                     "qk_first" if d == 0 else "kg_ready")

            def level_out(n, level):
                waits("level", n + 1)
                base = 2 * (n % 2)
                if level < LEVELS:
                    mask = C("levels")[:, P * level:P * level + P].bitcast(I32)
                    for t in range(NT):
                        link(dve.copy_predicated(AT[:, t, :, P * t:P * t + P],
                                                 mask.unsqueeze(1).broadcast_to([P, HEADS, P]),
                                                 ps[:, base + t, :].rearrange("p (h x) -> p h x", h=HEADS)),
                             "dve_step" if t == 0 else "level_out")
                else:
                    for d in range(2):
                        link(dve.tensor_copy(AT[:, d, :, P * (1 - d):P * (1 - d) + P],
                                             ps[:, base + d, :].rearrange("p (h x) -> p h x", h=HEADS)),
                             "dve_step" if d == 0 else "level_out")

            cur = FG.rearrange("p g t -> p (g t)")
            nxt = [TA, TB]
            for n in range(LEVELS):
                level_out(n, LEVELS - 1 if n == 0 else n - 1)
                waits("level", n + 2)
                m = 1 << n

                def halves(a, d):
                    return a[:, 4 * d:4 * d + 4, :].rearrange("p g (b two m) -> p (g b) two m", two=2, m=m)

                nb = T // m
                pair = cur[:, 0:8 * nb].rearrange("p (x two) -> p x two", two=2)
                for a, side in ((KG, 0), (QG, 1)) if n < LEVELS - 1 else ((QG, 1),):
                    for d in range(2):
                        s = side ^ d
                        v = halves(a, d)[:, :, s, :]
                        tot = pair[:, 2 * nb * d:2 * nb * d + 2 * nb, 1 - s]
                        link(tt(v, v, tot.unsqueeze(2).broadcast_to([P, 2 * nb, m]), ALU.mult),
                             "qk_ready" if a is QG and d == 1 else "dve_step")
                if n < LEVELS - 1:
                    o = nxt[n % 2][:, 0:4 * nb]
                    link(tt(o, pair[:, :, 0], pair[:, :, 1], ALU.mult))
                    cur = o
                if n in (3, 5, 7):
                    mod_in(n // 2)
            level_out(LEVELS, LEVELS)

            waits("o_done", 1)
            O = ar(2 * K1, HEADS, T)
            link(dve.tensor_copy(O, ps[:, 0:4, 0:T]))
            link(tt(SQ[:, 0:4, :], O, O, ALU.mult), "o_squared")
            waits("o_summed", 1)
            link(ts(rs[:, :], ps[:, 4:6, :].rearrange("p a b -> p (a b)"), 1.0 / P, EPS, ALU.mult, ALU.add), "o_mean")
            waits("o_rooted", 1)
            link(dve.reciprocal(rs[:, :], rs[:, :]))
            link(tt(O, O, rs[:, :].rearrange("p (h t) -> p h t", h=HEADS), ALU.mult))
            for h in range(HEADS):
                link(stt(CAT[:, HEADS + h, :], O[:, h, :], V("g_rec", h), SG[:, h, :], ALU.mult, ALU.mult),
                     "rec_ready" if h == HEADS - 1 else "dve_step")
            residual(out1)
            rms(X, V("g_ffn", 0, 8), mod[:, 1, 8:16])

            waits("logits", 1)
            lgt = ps[:, 5, 0:32].rearrange("p (t e) -> p t e", t=NT)
            waits("modulated", 3 * KD)
            link(dve.tensor_copy(AFF, lgt), "logits_read")
            link(dve.tensor_reduce(small[:, 38:40], AFF, AX_X, ALU.max))
            link(ts(small[:, 40:42], small[:, 38:40], -1.0, None, ALU.mult), "logit_max")
            waits("aff_exp", 2)
            link(dve.reciprocal(small[:, 38:40], small[:, 42:44]))
            for t in range(NT):
                link(ts(AFF[:, t, :], AFF[:, t, :], small[:, 38 + t:39 + t], None, ALU.mult),
                     "dve_step" if t == 0 else "aff")
            waits("aff_turned", 1)
            work, mask, pos, one = WORK[0:16, :], MASK[0:16, :], POS[0:16, :], ONE[0:16, :]
            link(dve.tensor_copy(work, ps[0:16, 5, 0:T]))
            link(dve.memset(one, 1.0))
            for _ in range(SLOTS // 8):
                link(dve.max(small[0:16, 0:8], work))
                link(dve.match_replace(work, small[0:16, 0:8], work, -1.0))
            link(ts(mask, work, 0.0, None, ALU.is_lt))
            link(dve.tensor_tensor_scan(pos, one, mask, 0.0, ALU.mult, ALU.add))
            link(tt(pos, pos, mask, ALU.mult), "pos")
            mod_in(4)
            waits("pos_turned", 1)
            link(dve.tensor_copy(POST, ps[:, 5, 0:32].rearrange("p (t e) -> p t e", t=NT)))
            for t in range(NT):
                link(tt(SEL[:, t, :, :], POST[:, t, :].unsqueeze(2).broadcast_to([P, EXPERTS, SLOTS]),
                        C("slots").unsqueeze(1).broadcast_to([P, EXPERTS, SLOTS]), ALU.is_equal),
                     "dve_step" if t == 0 else "sel")
            for t in range(NT):
                link(tt(PG[:, t, :, :], SEL[:, t, :, :], AFF[:, t, :].unsqueeze(2).broadcast_to([P, EXPERTS, SLOTS]),
                        ALU.mult), "dve_step" if t == 0 else "gated")
            mod_in(5)
            waits("rel_in", 32)
            link(dve.tensor_copy(RELB[0:33, :, :], REL[0:33, :].unsqueeze(2).broadcast_to([33, ATT, P])), "relb")
            link(dve.memset(MOE, 0.0), "acc_done")
            dve.sem_inc(S("hid_done"), 1)

            moe = MOE.rearrange("p (j i) t -> p j (i t)", j=CG)
            with dve.Fori(0, EXPERTS) as e:
                waits("sil", e + 1)
                waits("unit_used", e * EXP_UNITS + (exp0 + 16))
                tt(HID.rearrange("p (i f) -> p i f", i=2), SIL, ps[:, 2:4, 0:FJ // 2], ALU.mult).then_inc(S("hid_done"), 1)
                waits("hid_done", e + 2)
                dve.transpose(HIDT, HID.rearrange("p (q c) -> p c q", c=FC)).then_inc(S("hid_t"), 1)
                waits("scattered", e + 2)
                tt(moe, moe, ps[:, 4:8, :], ALU.add).then_inc(S("acc_done"), 1)
                waits("acc_done", e + 2)

            waits("moe_gated", KD)
            link(tt(X, X, SQ, ALU.add))
            rms(X, V("g_final", 0, 8), then="scaled")
            waits("scaled", KD)
            rms(X, V("g_mix_2", 0, 8), mod[:, 2, 8:16])

            waits("sgu_in", 48)
            link(tt(WS, WS, C("tri").unsqueeze(1).broadcast_to([P, ATT, P]), ALU.mult))
            waits("vs_sq", 2)
            link(ts(small[:, 44:46], small[:, 44:46], 1.0 / 512, EPS, ALU.mult, ALU.add), "vs_mean")
            waits("vs_rooted", 1)
            link(dve.reciprocal(small[:, 44:46], small[:, 44:46]))
            for t in range(NT):
                link(stt(VSN[:, t, :], VS[:, t, :], small[:, 44 + t:45 + t], GS, ALU.mult, ALU.mult),
                     "dve_step" if t == 0 else "vsn")

            heads = [0]

            def softmax(bias, ao_out):
                def max_of(h):
                    n = heads[0] + h
                    waits("scores", n + 1)
                    if n >= 2:
                        waits("pt", n - 1)
                    s, b = SC[:, n % 2, :], 2 * (n % 2)
                    link(tt(s, ps[:, 4 + n % 2, :], bias(h), ALU.add), "scores_read")
                    link(dve.tensor_reduce(small[:, 56 + b:58 + b], s.rearrange("p (t k) -> p t k", t=NT), AX_X, ALU.max))
                    link(ts(small[:, 48 + b:50 + b], small[:, 56 + b:58 + b], -1.0, None, ALU.mult), "row_max")

                def divide(h):
                    n = heads[0] + h
                    b = 2 * (n % 2)
                    waits("p_exp", NT * (n + 1))
                    link(dve.reciprocal(small[:, 56 + b:58 + b], small[:, 52 + b:54 + b]))
                    for t in range(NT):
                        s = SC[:, n % 2, T * t:T * t + T]
                        link(ts(s, s, small[:, 56 + b + t:57 + b + t], None, ALU.mult), "dve_step" if t == 0 else "probs")

                def pair_out(c):
                    waits("ao", heads[0] + 2 * c + 2)
                    link(ao_out(c), "ao_out")

                max_of(0)
                for h in range(ATT):
                    if h + 1 < ATT:
                        max_of(h + 1)
                    divide(h)
                    if h >= 2 and h % 2 == 0:
                        pair_out(h // 2 - 1)
                pair_out(ATT // 2 - 1)
                heads[0] += ATT

            softmax(lambda h: C("causal"), lambda c: dve.tensor_copy(AO[:, c, :], ps[:, 7, 0:T]))
            waits("sgu", 1)
            link(tt(SGO.rearrange("p c (t x) -> p c t x", t=NT), ps[:, 0:4, 0:T].rearrange("p c (t x) -> p c t x", t=NT),
                    BS.unsqueeze(2).broadcast_to([P, 4, NT, P]), ALU.add))
            link(tt(SGO, SGO, UA, ALU.mult), "sgo")
            waits("evacuated", proj2[-1]["items"][-1]["b"] + 1)
            link(tt(GA, GA, SQ, ALU.mult))
            link(tt(GB, GB, XN, ALU.mult))
            link(tt(MG, GA, GB, ALU.add), "merged")
            residual(out2)
            rms(X, V("g_ffn_2", 0, 8), mod[:, 3, 8:16])
            for g in ff1:
                for it in g["items"]:
                    waits("evacuated", it["b"] + 1)
                    h = HFF[:, it["n"], :]
                    link(tt(h, h, h, ALU.mult), "ff_squared")
            residual(ff2)
            rms(X, V("g_final_2", 0, 8), then="scaled")
            waits("scaled", 2 * KD)
            waits("bias_in", 32)
            for l in range(LAYERS3):
                rms(X, V("pre_norm_g_3", 8 * l, 8), mod[:, 4 + l, 8:16])
                waits("evacuated", in3[l][-1]["items"][-1]["b"] + 1)
                softmax(lambda h: BIAS[:, h, :],
                        lambda c: tt(CAT3[:, c, :], ps[:, 7, 0:T], HQ[:, c, :], ALU.mult))
                waits("evacuated", out3[l][-1]["items"][-1]["b"] + 1)
                rms(MIX3, V("post_norm_g_3", 8 * l, 8), times=mod[:, 4 + l, 16:24], then="scaled")
                waits("scaled", (3 + l) * KD)
                link(tt(X, X, SQ, ALU.add), "x_updated" if l < LAYERS3 - 1 else "x_final")

        @block.gpsimd
        def _(pool):
            made = {}

            def link(ins, name="pool_step"):
                made[name] = made.get(name, 0) + 1
                ins.then_inc(S(name), 1)
                pool.wait_ge(S(name), made[name])

            pool.wait_ge(S("lb_ready"), 1)
            pool.wait_ge(S("evacuated"), in1[-1]["items"][-1]["b"] + 1)
            for g in range(8):
                link(pool.tensor_scalar(FGC[:, g, :], FGC[:, g, :], small[:, 8 + g:9 + g], small[:, g:g + 1],
                                        ALU.mult, ALU.add))
            link(pool.tensor_scalar(KGC, FGC, -1.0, 1.0, ALU.mult, ALU.add))
            cur = FGC.rearrange("p g t -> p (g t)")
            nxt = [TAC, TBC]
            for n in range(LEVELS):
                m = 1 << n
                nb = T // m
                pair = cur[:, 0:8 * nb].rearrange("p (x two) -> p x two", two=2)
                for d in range(2):
                    v = KGC[:, 4 * d:4 * d + 4, :].rearrange("p g (b two m) -> p (g b) two m", two=2, m=m)[:, :, d, :]
                    tot = pair[:, 2 * nb * d:2 * nb * d + 2 * nb, 1 - d]
                    link(pool.tensor_tensor(v, v, tot.unsqueeze(2).broadcast_to([P, 2 * nb, m]), ALU.mult),
                         "kgc_ready" if n == LEVELS - 1 and d == 1 else "pool_step")
                if n < LEVELS - 1:
                    o = nxt[n % 2][:, 0:4 * nb]
                    link(pool.tensor_tensor(o, pair[:, :, 0], pair[:, :, 1], ALU.mult))
                    cur = o
            pool.wait_ge(S("gated"), 1)
            for e in range(EXPERTS):
                if e >= 2:
                    pool.wait_ge(S("pgt"), e - 1)
                link(pool.tensor_copy(PG4[e % 2].rearrange("p t (j s) -> p t j s", j=CG),
                                      PG[:, :, e, :].unsqueeze(2).broadcast_to([P, NT, CG, SLOTS])), "pg4")
            pool.wait_ge(S("xs_out"), KD)
            pool.wait_ge(S("pgt_out"), EXPERTS)
            xs = XS.rearrange("p k (e s) -> p k e s", e=EXPERTS)
            with pool.Fori(0, EXPERTS) as e:
                pool.wait_ge(S("unit_used"), e * EXP_UNITS + (exp0 - 8))
                pool.tensor_copy(XCUR, xs[:, :, e, :]).then_inc(S("xcur"), 1)
                pool.wait_ge(S("scattered"), e + 1)
                pool.tensor_copy(PGCUR, PGT[:, e, :]).then_inc(S("pgcur"), 1)
            for l in range(LAYERS3):
                pool.wait_ge(S("evacuated"), in3[l][-1]["items"][-1]["b"] + 1)
                if l == 0:
                    link(pool.memset(ZP, 0.0))
                link(pool.tensor_tensor(ZP[:, :, 1:T + 1], CC, CU, ALU.mult))
                for c in range(4):
                    w = [V("conv_w_3", 12 * l + 4 * k + c) for k in range(3)]
                    y = CAT3[:, 4 + c, :]
                    link(pool.tensor_scalar(y, ZP[:, c, 0:T], w[0], None, ALU.mult))
                    for k in (1, 2):
                        link(pool.tensor_scalar(CC[:, c, :], ZP[:, c, k:k + T], w[k], None, ALU.mult))
                        link(pool.tensor_tensor(y, y, CC[:, c, :], ALU.add))
                link(pool.tensor_tensor(CB, CB, CS, ALU.mult))
                link(pool.tensor_tensor(CAT3[:, 4:8, :], CAT3[:, 4:8, :], CB, ALU.mult), "conv")



def kernel(**inputs):
    import concourse.bacc as _bacc
    from concourse.bass_utils import run_bass_kernel_spmd as _run

    a = {k: np.asarray(v) for k, v in inputs.items()}

    def feature_major(x):
        return np.ascontiguousarray(x.reshape(T, KD, P).transpose(2, 1, 0))

    names = {n: n for n, _ in VECTORS}
    vec = np.concatenate([a[n].reshape(-1, P).T for n in names], 1)
    const, offsets = constants()
    arrays = {
        "xT": feature_major(a["x"]), "ctxT": feature_major(a["ctx"]),
        "vec": np.ascontiguousarray(vec), "const": const, "offsets": offsets,
        "rel": np.concatenate([a["rel_bias_3"], np.ones((1, ATT), np.float32)], 0),
        "w_sgu": np.ascontiguousarray(a["w_sgu_2"][0].transpose(2, 0, 1)),
        "g_sgu": np.ascontiguousarray(np.broadcast_to(a["g_sgu_2"], (P, 512))),
        "b_sgu": np.ascontiguousarray(np.repeat(a["b_sgu_2"][0].reshape(4, 2, 1, P), 64, 2).reshape(4, P, P)
                                      .transpose(1, 0, 2)),
    }
    for n in ("w_ada", "w_in", "w_fourier", "w_out", "w_router", "w_exp_gate", "w_exp_up", "w_exp_down", "w_ada_2",
              "w_in_2", "w_proj_attn_2", "w_proj_sgu_2", "w_out_2", "w_ff1_2", "w_ff2_2", "w_ada_3", "w_in_3",
              "w_out_3"):
        arrays[n] = np.ascontiguousarray(a[n])
    nc = _bacc.Bacc("TRN2", target_bir_lowering=False, num_devices=1)
    inp = {n: nc.dram_tensor("in_" + n, v.shape, mybir.dt.from_np(v.dtype), kind="ExternalInput").ap()
           for n, v in arrays.items()}
    scratch = nc.dram_tensor("bias_rows", (ATT, 129 * 512), F32).ap()
    out = nc.dram_tensor("out_xT", (P, KD, T), F32, kind="ExternalOutput").ap()
    build(nc, inp, scratch, out)
    r = _run(nc, [{"in_" + n: v for n, v in arrays.items()}], core_ids=[0])
    return np.ascontiguousarray(r.results[0]["out_xT"].transpose(2, 1, 0).reshape(1, T, D))
```

```python
from contextlib import ExitStack

import numpy as np

import concourse.bass as bass
from concourse import mybir

F32 = mybir.dt.float32
F32R = mybir.dt.float32r
I32 = mybir.dt.int32
ALU = mybir.AluOpType
ACT = mybir.ActivationFunctionType
AX_X = mybir.AxisListType.X

P = 128
T = 256
NT = T // P
D = 1024
KD = D // P
EPS = 1e-6
HEADS = 4
EXPERTS = 16
SLOTS = 2 * T // EXPERTS
F_EXP = 2816
CG = 4
FJ = F_EXP // CG
FC = F_EXP // P
ATT = 8
FF = 4096
LAYERS3 = 2
NEG = -1e30

WCOL = 384
UNIT = KD * WCOL
RING = 4
HI = 4
ADA_PASS = 3072
ADA_J = ADA_PASS // CG
EXP_UNITS = 24
LEVELS = 8

VECTORS = [("c", 8), ("c_ctx", 8), ("c_2", 8), ("c_3", 8), ("b_ada", 48), ("g_mix", 8), ("lb_logits", 16),
           ("g_rec", 4), ("g_ffn", 8), ("g_final", 8), ("b_ada_2", 48), ("g_mix_2", 8), ("g_ffn_2", 8),
           ("g_final_2", 8), ("b_ada_3", 48), ("pre_norm_g_3", 16), ("post_norm_g_3", 16), ("conv_w_3", 24)]
VCOL = {}
_at = 0
for _n, _k in VECTORS:
    VCOL[_n] = _at
    _at += _k
NVEC = _at

CONSTS = [("ident", 128), ("ones", 128), ("dft_feat", 256), ("dft_cos", 512), ("dft_sin", 512),
          ("causal", 512), ("tri", 128), ("slots", 32), ("levels", LEVELS * 128)]
CCOL = {}
_at = 0
for _n, _k in CONSTS:
    CCOL[_n] = (_at, _k)
    _at += _k
NCONST = _at


def constants():
    out = np.zeros((P, NCONST), np.float32)

    def put(name, a):
        at, k = CCOL[name]
        out[:, at:at + k] = np.asarray(a).reshape(P, k)

    i = np.arange(P)
    t = np.arange(T)
    put("ident", np.eye(P))
    put("ones", np.ones((P, P)))
    ang = 2 * np.pi * (np.outer(i, i) % P) / P
    put("dft_feat", np.concatenate([np.cos(ang), np.sin(ang)], 1))
    ang = 2 * np.pi * (np.outer(t, t) % T) / T
    norm = 1 / np.sqrt(T * P)
    put("dft_cos", (np.cos(ang) * norm).reshape(NT, P, T).transpose(1, 0, 2))
    put("dft_sin", (-np.sin(ang) * norm).reshape(NT, P, T).transpose(1, 0, 2))
    put("causal", np.where(t[None, :] <= t[:, None], 0.0, NEG).reshape(NT, P, T).transpose(1, 0, 2))
    put("tri", (i[:, None] <= i[None, :]).astype(np.float32))
    put("slots", np.broadcast_to(np.arange(1, SLOTS + 1), (P, SLOTS)))
    lv = np.zeros((P, LEVELS, P))
    for n in range(LEVELS - 1):
        m = 1 << n
        a, b = i[:, None], i[None, :]
        lv[:, n] = (a // (2 * m) == b // (2 * m)) & (a // m != b // m)
    lv[:, LEVELS - 1] = np.eye(P)
    put("levels", lv)
    off = np.arange(-(T - 1), T)
    n = np.abs(off)
    large = 8 + (np.log(np.maximum(n, 1).astype(np.float32) / np.float32(8)) / np.float32(np.log(128.0))
                 * np.float32(8)).astype(np.int32)
    bucket = np.where(off > 0, 16, 0) + np.where(n < 8, n, np.minimum(large, 15))
    count = sum(((n <= w // 2) & (n % d == 0)).astype(int) for w, d in ((128, 1), (512, 4), (2048, 16)))
    offsets = np.zeros((33, 512), np.float32)
    offsets[bucket, np.arange(off.size)] = 1.0
    offsets[32, :off.size] = np.where(count > 0, np.log(np.maximum(count, 1)), NEG)
    return out, offsets


BROW_EVERY = 3
QKV = 4 + 4 + 2


class Plan:

    def __init__(self):
        self.n = 0
        self.ready = {}
        self.fill = [0] * RING
        self.blocks = 0
        self.inner = 0
        self.splits = []

    def unit(self, dmas=1):
        u = self.n
        self.n += 1
        self.fill[u % RING] += 16 * dmas
        self.ready[u] = self.fill[u % RING]
        return u

    def block(self, u, last, **kw):
        b = self.blocks
        self.blocks += 1
        return dict(u=u, b=b, last=last, done=self.step(u, last), **kw)

    def step(self, u, last):
        if last:
            return "unit_used", u + 1
        self.inner += 1
        return "block_done", self.inner

    def split(self, u, col, w, done=None):
        self.splits.append(dict(u=u, col=col, w=w, done=done))
        return len(self.splits) - 1

    def dense(self, cols, kinds, turned=(), after=lambda i: None):
        units = []
        n = 0
        while n < cols // P:
            inside = any(a <= n < b for a, b in turned)
            end = min([cols // P] + [a for a, _ in turned if a > n])
            k = 2 if inside else min(WCOL // P, end - n)
            u = self.unit()
            todo = [(n, which) for which in kinds(n)] if inside else \
                [(i, which) for i in range(n, n + k) for which in kinds(i)]
            at = [self.split(u, i * P, k * P) for i in range(k)]
            assert not inside or at[0] % 2 == 0
            items = [self.block(u, i == len(todo) - 1, n=m, turned=inside, src=which, col=(m - n) * P, s=at[m - n])
                     for i, (m, which) in enumerate(todo)]
            for it in items:
                for j in range(2 if inside else 1):
                    self.splits[it["s"] + j]["done"] = it["done"]
            units.append(dict(u=u, c0=n * P, w=k * P, items=items))
            after(len(units) - 1)
            n += k
        return units


def shares(units):
    n = sum(len(g["items"]) for g in units) - QKV
    return [((n + ATT - 1 - h) // ATT - 1, 1) for h in range(ATT)]


def out_by(units, n):
    return 1 + max(it["b"] for g in units for it in g["items"] if it["n"] <= n < it["n"] + (2 if it["turned"] else 1))


def build(nc, inp, scratch, out):
    plan = Plan()
    ada = [[plan.unit() for _ in range(KD)]]

    ada.append([])

    def ada_after(i):
        if i < KD:
            ada[1].append(plan.unit())

    in1 = plan.dense(3072, lambda n: ["lat", "ctx"] if 8 <= n < 20 else ["lat"], [(8, 12)], ada_after)
    assert len(ada[1]) == KD
    ada += [[plan.unit() for _ in range(KD)] for _ in range(2)]
    out1 = plan.dense(D, lambda n: ["cat"])
    ada += [[plan.unit() for _ in range(KD)] for _ in range(2)]
    exp0 = plan.n
    for _ in range(EXPERTS * EXP_UNITS):
        plan.unit()
    assert EXP_UNITS % RING == 0
    in2 = plan.dense(4608, lambda n: ["lat"], [(8, 12), (16, 20)])
    proj2 = []
    for c0 in range(0, D, WCOL):
        w = min(WCOL, D - c0)
        u = plan.unit(2)
        ns = range(c0 // P, (c0 + w) // P)
        proj2.append(dict(u=u, c0=c0, w=w, items=[
            plan.block(u, n == ns[-1] and s == 1, n=n, col=n * P - c0, src=s) for s in (0, 1) for n in ns]))
    out2 = plan.dense(D, lambda n: ["merged"])
    ff1 = plan.dense(FF, lambda n: ["lat"])
    ff2 = []
    for c0 in range(0, D, WCOL):
        w = min(WCOL, D - c0)
        us = [plan.unit() for _ in range(FF // D)]
        ns = range(c0 // P, (c0 + w) // P)
        at = []
        for u in us:
            at.append([])
            for n in ns:
                if u == us[-1]:
                    it = plan.block(u, n == ns[-1], n=n, col=n * P - c0)
                    at[-1].append((it, plan.split(u, n * P - c0, w, it["done"])))
                else:
                    at[-1].append((None, plan.split(u, n * P - c0, w, plan.step(u, n == ns[-1]))))
        ff2.append(dict(us=us, c0=c0, w=w, at=at, items=[it for it, _ in at[-1]]))
    in3, out3 = [], []
    for _ in range(LAYERS3):
        in3.append(plan.dense(FF, lambda n: ["lat"], [(8, 12)]))
        out3.append(plan.dense(D, lambda n: ["cat"]))
    starts = {"in1": in1[0]["items"][0]["s"], "out1": out1[0]["items"][0]["s"], "in2": in2[0]["items"][0]["s"],
              "out2": out2[0]["items"][0]["s"], "end": len(plan.splits)}

    ctx = ExitStack()
    with ctx:
        sems = {}

        def S(name):
            if name not in sems:
                sems[name] = ctx.enter_context(nc.semaphore(name))
            return sems[name]

        w_ready = [S(f"w_ready{i}") for i in range(RING)]

        def sb(name, shape, dt=F32):
            return ctx.enter_context(nc.sbuf_tensor(name, shape, dt))[:]

        with nc.sbuf_tensor("ring", [P, RING, UNIT], F32) as ring_t:
            ring = ring_t[:]
        ring_lo = sb("ring_lo", [P, RING, UNIT], F32R)
        w_hi = sb("w_hi", [P, HI, KD, P], F32R)
        X = sb("X", [P, KD, T])
        vec = sb("vec", [P, NVEC])
        const = sb("const", [P, NCONST])
        conds = sb("conds", [P, KD, 32])
        rows = sb("rows", [P, 2, ADA_J // 2])
        mod = sb("mod", [P, 6, 24])
        modc = sb("modc", [P, 24])
        scl = sb("scl", [P, 8, 8])
        rs = sb("rs", [P, HEADS * T])
        small = sb("small", [P, 64])
        WR = sb("WR", [P, KD, EXPERTS])

        def arena_parts(name, at, n):
            with nc.sbuf_tensor(name + "_before", [P, at], F32):
                with nc.sbuf_tensor(name, [P, n], F32R) as part:
                    return part[:]

        x_parts = arena_parts("x_parts", 2 * 1024, 4 * 1024)
        ctx_parts = arena_parts("ctx_parts", 6 * 1024, 4 * 1024)
        ff_parts = arena_parts("ff_parts", 8 * 1024, 16 * 1024)
        arena = sb("arena", [P, 26 * 1024])
        ps = ctx.enter_context(nc.psum_tensor("ps", [P, 8, 512], F32))

        def ar(at, *shape):
            n = 1
            for s in shape:
                n *= s
            a = arena[:, at:at + n]
            if len(shape) == 2:
                a = a.rearrange("p (a b) -> p a b", a=shape[0])
            if len(shape) == 3:
                a = a.rearrange("p (a b c) -> p a b c", a=shape[0], b=shape[1])
            return a

        def C(name):
            at, k = CCOL[name]
            return const[:, at:at + k]

        ident, ones = C("ident"), C("ones")

        def V(name, n=0, k=1):
            return vec[:, VCOL[name] + n:VCOL[name] + n + k]

        K1 = 1024
        SQ = ar(0, KD, T)
        XN = ar(2 * K1, KD, T)
        H = ar(4 * K1, KD, T)
        CTX = ar(6 * K1, KD, T)
        HC = ar(8 * K1, KD, T)
        FG = ar(10 * K1, 8, T)
        KG = ar(12 * K1, 8, T)
        FGC = ar(14 * K1, 8, T)
        KGC = ar(16 * K1, 8, T)
        U = ar(18 * K1, HEADS, T)
        Q = ar(19 * K1, HEADS, T)
        VT = ar(20 * K1, NT, 512)
        VC = ar(21 * K1, NT, 512)
        SG = ar(22 * K1, HEADS, T)
        TA = ar(23 * K1, 1024)
        TB = ar(24 * K1, 512)
        TAC = ar(8 * K1, 1024)
        TBC = ar(9 * K1, 512)
        DFT = ar(2 * K1, NT, HEADS, T)
        QG = ar(0, 8, T)
        AT = ar(6 * K1, NT, HEADS, T)
        KT = ar(8 * K1, NT, 8, P)
        S0 = ar(14 * K1, 8, P)
        ROOTS = ar(0, NT * HEADS, P)
        CAT = ar(4 * K1, KD, T)
        Z = ar(18 * K1, HEADS, T)
        WF = ar(24 * K1 + 512, HEADS, P)
        HTOK = ar(6 * K1, NT, D)
        XS = ar(8 * K1, KD, EXPERTS * SLOTS)
        PG = ar(16 * K1, NT, EXPERTS, CG * SLOTS)
        SEL = ar(1 * K1, NT, EXPERTS, SLOTS)
        PGT = ar(12 * K1, EXPERTS, T)
        SIL = ar(16 * K1, 2, FJ // 2)
        HID = ar(17 * K1, FJ)
        HIDT = ar(18 * K1, FC, SLOTS)
        YE = ar(19 * K1, 256)
        XCUR = ar(19 * K1 + 256, KD, SLOTS)
        PGCUR = ar(19 * K1 + 512, T)
        MOE = ar(2 * K1, KD, T)
        AFFT = ar(21 * K1, T)
        WORK = ar(21 * K1 + 256, T)
        MASK = ar(21 * K1 + 512, T)
        POS = ar(21 * K1 + 768, T)
        AFF = ar(22 * K1, NT, EXPERTS)
        POST = ar(22 * K1 + 32, NT, EXPERTS)
        ONE = ar(22 * K1 + 256, T)
        RELB = ar(23 * K1, ATT, P)
        OFFS = ar(24 * K1, 512)
        REL = ar(22 * K1, ATT)
        BROW = ar(25 * K1, 2, 512)
        QA = ar(6 * K1, 4, T)
        KA = ar(7 * K1, 4, T)
        VA = ar(8 * K1, NT, 512)
        UA = ar(9 * K1, 4, T)
        VS = ar(10 * K1, NT, 512)
        GA = ar(11 * K1, KD, T)
        GB = ar(13 * K1, KD, T)
        SC = ar(15 * K1, 2, 512)
        PT = ar(16 * K1, 2, 512)
        AO = ar(17 * K1, 4, T)
        SGO = ar(18 * K1, 4, T)
        VSN = ar(19 * K1, NT, 512)
        WS = ar(20 * K1, ATT, P)
        GS = ar(21 * K1, 512)
        BS = ar(21 * K1 + 512, 4, P)
        MG = H
        HFF = ar(8 * K1, FF // P, T)
        HQ = ar(9 * K1, 4, T)
        CU = ar(10 * K1, 4, T)
        CB = ar(11 * K1, 4, T)
        CC = ar(12 * K1, 4, T)
        CS = ar(13 * K1, 4, T)
        ZP = ar(22 * K1, 4, T + 2)
        BIAS = ar(18 * K1, ATT, NT * T)
        MIX3 = ar(15 * K1, KD, T)
        CAT3 = ar(24 * K1, KD, T)

        X_HI = x_parts[:, 0:2 * K1].rearrange("p (k t) -> p k t", k=KD)
        X_LO = x_parts[:, 2 * K1:4 * K1].rearrange("p (k t) -> p k t", k=KD)
        C_HI = ctx_parts[:, 0:2 * K1].rearrange("p (k t) -> p k t", k=KD)
        C_LO = ctx_parts[:, 2 * K1:4 * K1].rearrange("p (k t) -> p k t", k=KD)
        FF_LO = ff_parts[:, 0:8 * K1].rearrange("p (k t) -> p k t", k=FF // P)
        FF_HI = ff_parts[:, 8 * K1:16 * K1].rearrange("p (k t) -> p k t", k=FF // P)

        def slot(u, *shape, of=ring):
            n = 1
            for s in shape:
                n *= s
            a = of[:, u % RING, 0:n]
            if len(shape) == 2:
                return a.rearrange("p (a b) -> p a b", a=shape[0])
            if len(shape) == 3:
                return a.rearrange("p (a b c) -> p a b c", a=shape[0], b=shape[1])
            return a

        def gate_selection(eng, t):
            full = [P, EXPERTS, CG, SLOTS]
            eng.tensor_tensor(PG[:, t, :, :].rearrange("p e (j s) -> p e j s", j=CG),
                              SEL[:, t, :, :].unsqueeze(2).broadcast_to(full),
                              AFF[:, t, :].unsqueeze(2).unsqueeze(3).broadcast_to(full),
                              ALU.mult).then_inc(S(f"gated{t}"), 1)

        block = ctx.enter_context(nc.Block())

        @block.sync
        def _(sp):
            def load(u, dst, src):
                if u >= RING:
                    sp.wait_ge(S("unit_used"), u - RING + 1)
                sp.dma_start(dst, src).then_inc(w_ready[u % RING], 16)

            def load_ada(p, which=range(KD)):
                w, h = [(inp["w_ada"][0], 0), (inp["w_ada"][0], 1), (inp["w_ada_2"][0], 0),
                        (inp["w_ada_2"][0], 1), (inp["w_ada_3"][0], 0), (inp["w_ada_3"][1], 0)][p]
                for kc in which:
                    u = ada[p][kc]
                    load(u, slot(u, ADA_PASS), w[kc * P:(kc + 1) * P, h * ADA_PASS:(h + 1) * ADA_PASS])

            def load_dense(units, w, after=lambda i: None):
                view = w.rearrange("(k p) n -> p k n", p=P)
                for i, g in enumerate(units):
                    load(g["u"], slot(g["u"], KD, g["w"]), view[:, :, g["c0"]:g["c0"] + g["w"]])
                    after(i)

            sp.dma_start(X[:], inp["xT"]).then_inc(S("x_in"), 16)
            sp.dma_start(vec[:], inp["vec"]).then_inc(S("vec_in"), 16)
            sp.dma_start(const[:, 0:2 * P], inp["const"][:, 0:2 * P]).then_inc(S("small_in"), 16)
            sp.dma_start(CTX, inp["ctxT"]).then_inc(S("x_in"), 16)
            sp.dma_start(REL[0:33, :], inp["rel"]).then_inc(S("rel_in"), 16)
            sp.dma_start(OFFS[0:33, :], inp["offsets"]).then_inc(S("rel_in"), 16)
            load_ada(0)

            def after_in1(i):
                if i < KD:
                    load_ada(1, [i])
                if i == 2:
                    sp.dma_start(const[:, 2 * P:], inp["const"][:, 2 * P:]).then_inc(S("const_in"), 16)
                    sp.dma_start(WF, inp["w_fourier"][0].rearrange("g c d -> c g d")).then_inc(S("late_in"), 16)
                    sp.dma_start(WR[:], inp["w_router"][0].rearrange("(k p) e -> p k e", p=P)).then_inc(S("late_in"), 16)

            load_dense(in1, inp["w_in"][0], after_in1)
            for p in (2, 3):
                load_ada(p)
            load_dense(out1, inp["w_out"][0])
            for p in (4, 5):
                load_ada(p)

            gate = inp["w_exp_gate"].rearrange("a e (k p) f -> (a e) p k f", p=P)
            up = inp["w_exp_up"].rearrange("a e (k p) f -> (a e) p k f", p=P)
            down = inp["w_exp_down"].rearrange("a e (p c) d -> (a e) p (c d)", p=P)
            with sp.Fori(0, EXPERTS) as e:
                for k in range(EXP_UNITS):
                    sp.wait_ge(S("unit_used"), e * EXP_UNITS + (exp0 + k - RING + 1))
                    s = (exp0 + k) % RING
                    if k < 16:
                        src = (gate if k < 8 else up)[e, :, k % 8, :]
                        dst = ring[:, s, 0:F_EXP]
                    else:
                        c0 = 3 * (k - 16)
                        c1 = min(c0 + 3, FC)
                        src = down[e, :, c0 * D:c1 * D]
                        dst = ring[:, s, 0:(c1 - c0) * D]
                    sp.dma_start(dst, src).then_inc(w_ready[s], 16)

            load_dense(in2, inp["w_in_2"][0])
            pa = inp["w_proj_attn_2"][0].rearrange("(k p) n -> p k n", p=P)
            pb = inp["w_proj_sgu_2"][0].rearrange("(k p) n -> p k n", p=P)
            for g in proj2:
                dst = slot(g["u"], 2, 4, g["w"])
                load(g["u"], dst[:, 0], pa[:, :, g["c0"]:g["c0"] + g["w"]])
                load(g["u"], dst[:, 1], pb[:, :, g["c0"]:g["c0"] + g["w"]])
            load_dense(out2, inp["w_out_2"][0])
            load_dense(ff1, inp["w_ff1_2"][0])
            v = inp["w_ff2_2"][0].rearrange("(b k p) n -> b p k n", b=FF // D, p=P)
            for g in ff2:
                for b, u in enumerate(g["us"]):
                    load(u, slot(u, KD, g["w"]), v[b, :, :, g["c0"]:g["c0"] + g["w"]])
            for l in range(LAYERS3):
                load_dense(in3[l], inp["w_in_3"][l])
                load_dense(out3[l], inp["w_out_3"][l])
            sp.wait_ge(S("x_final"), KD)
            sp.dma_start(out, X[:]).then_inc(S("stored"), 16)
            sp.wait_ge(S("stored"), 16)

        @block.tensor
        def _(pe):
            def unit_ready(u):
                pe.wait_ge(w_ready[u % RING], plan.ready[u])

            def count(ins, name):
                ins.then_inc(S(name), 1)

            def ada_unit(p, kc):
                u = ada[p][kc]
                unit_ready(u)
                if kc == 0 and p > 0:
                    pe.wait_ge(S("rows_out"), p)
                for i in range(2):
                    for j in range(CG):
                        at = ADA_J * j + ADA_J // 2 * i
                        m = pe.matmul(ps[32 * j:32 * j + 32, 6 + i, 0:ADA_J // 2], conds[:, kc, :],
                                      ring[:, u % RING, at:at + ADA_J // 2], start=(kc == 0),
                                      stop=(kc == KD - 1), skip_group_check=True)
                count(m, "unit_used")

            def turn(p):
                pe.wait_ge(S("rows_out"), p + 1)
                if p > 0:
                    pe.wait_ge(S("mod_ready"), p)
                pick = ident.rearrange("p (j c) -> p j c", j=CG)[:, :, 0:4]
                for q in range(6):
                    m = pe.matmul(ps[:, 4, 16 * q:16 * q + 16], rows[:, q // 3, P * (q % 3):P * (q % 3) + P], pick,
                                  start=True, stop=True, skip_group_check=True)
                count(m, "turned")

            def parts(hi, lo, x_hi, x_lo):
                return (hi, x_hi), (lo, x_hi), (hi, x_lo)

            def dense_blocks(units, src, first, after=lambda i: None):
                for gi, g in enumerate(units):
                    lo = slot(g["u"], KD, g["w"], of=ring_lo)
                    for it in g["items"]:
                        pe.wait_ge(S("w_split"), it["s"] + (2 if it["turned"] else 1))
                        if it["b"] >= 4:
                            pe.wait_ge(S("evacuated"), it["b"] - 3)
                        bank = it["b"] % 4
                        h = src(it)
                        i = it["s"] % HI
                        for t in range(NT if it["turned"] else 1):
                            for k in range(KD):
                                if first is not None:
                                    pe.wait_ge(S("x_split"), first + k + 1)
                                if it["turned"]:
                                    x = [a[:, k, P * t:P * t + P] for a in h]
                                    for j, (w, a) in enumerate(parts(w_hi[:, i:i + 2, k, :], lo[:, k, :], *x)):
                                        m = pe.matmul(ps[:, bank, 2 * P * t:2 * P * t + 2 * P], a, w,
                                                      start=(k == 0 and j == 0), stop=(k == KD - 1 and j == 2))
                                else:
                                    x = [a[:, k, :] for a in h]
                                    wl = lo[:, k, it["col"]:it["col"] + P]
                                    for j, (w, a) in enumerate(parts(w_hi[:, i, k, :], wl, *x)):
                                        m = pe.matmul(ps[:, bank, 0:T], w, a, start=(k == 0 and j == 0),
                                                      stop=(k == KD - 1 and j == 2))
                            first = None
                        count(m, "unit_used" if it["last"] else "block_done")
                        if it["last"]:
                            after(gi)
                        yield

            def dense(units):
                for _ in dense_blocks(units, lambda it: (X_HI, X_LO), split_input()):
                    pass

            inputs_split = [0]

            def split_input():
                inputs_split[0] += KD
                return inputs_split[0] - KD

            norms = [0]

            def sum_squares(sq=SQ):
                norms[0] += 1
                for c in range(KD):
                    pe.wait_ge(S("squared"), KD * (norms[0] - 1) + c + 1)
                    m = pe.matmul(ps[:, 5, 0:T], ones, sq[:, c, :], start=(c == 0), stop=(c == KD - 1))
                count(m, "summed")

            pe.wait_ge(S("small_in"), 16)
            sum_squares()
            pe.wait_ge(S("conds_ready"), 1)
            for kc in range(2):
                ada_unit(0, kc)
            sum_squares()
            for kc in range(2, KD):
                ada_unit(0, kc)
            turn(0)
            lat = split_input()
            split_input()

            def in1_src(it):
                if it["src"] == "lat":
                    return X_HI, X_LO
                pe.wait_ge(S("x_split"), 2 * KD)
                return C_HI, C_LO

            rest = dense_blocks(in1, in1_src, lat, lambda i: ada_unit(1, i) if i < KD else None)
            pe.wait_ge(S("mod_ready"), 1)
            for h in range(ATT):
                for _ in range(BROW_EVERY):
                    next(rest)
                pe.wait_ge(S("relb"), 1)
                if h >= 2:
                    pe.wait_ge(S("brow_out"), h - 1)
                m = pe.matmul(ps[:, 4 + h % 2, 0:511], RELB[0:33, h, :], OFFS[0:33, 0:511], start=True, stop=True)
                count(m, "brow")
            for _ in rest:
                pass
            pe.wait_ge(S("brow_out"), ATT)
            turn(1)

            pe.wait_ge(S("evacuated"), in1[-1]["items"][-1]["b"] + 1)
            todo = [(2, k) for k in range(KD)] + [(3, k) for k in range(KD)]

            def fill(k):
                for _ in range(k):
                    if todo:
                        p, kc = todo.pop(0)
                        ada_unit(p, kc)
                        if kc == KD - 1:
                            turn(p)

            pe.wait_ge(S("const_in"), 16)
            for t in range(NT):
                for g in range(HEADS):
                    m = pe.matmul(ps[:, 2 * t + g // 2, T * (g % 2):T * (g % 2) + T], U[:, g, P * t:P * t + P],
                                  C("dft_feat"), start=True, stop=True)
            count(m, "dft_feat")
            fill(2)
            pe.wait_ge(S("dft_out"), 1)
            for g in range(HEADS):
                for i, w in enumerate(("dft_cos", "dft_sin")):
                    for t in range(NT):
                        m = pe.matmul(ps[:, g, 0:T], DFT[:, t, g, P * i:P * i + P], C(w)[:, T * t:T * t + T],
                                      start=(i == 0 and t == 0), stop=(i == 1 and t == 1))
            count(m, "dft_tok")
            pe.wait_ge(S("z_out"), 1)
            pe.wait_ge(S("late_in"), 32)
            for g in range(HEADS):
                m = pe.matmul(ps[:, g, 0:T], WF[:, g, :], Z[:, g, :], start=True, stop=True)
            count(m, "fourier")
            fill(1)

            pe.wait_ge(S("kg_ready"), 1)
            pe.wait_ge(S("fourier_out"), 1)
            for t in range(NT):
                for h in range(HEADS):
                    for d in range(2):
                        m = pe.matmul(ps[:, t, P * h:P * h + P], KG[:, 4 * d + h, P * t:P * t + P],
                                      Q[:, h, P * t:P * t + P], start=(d == 0), stop=(d == 1))
            count(m, "level")
            for n in range(LEVELS):
                if n >= 1:
                    pe.wait_ge(S("qk_ready"), n)
                    pe.wait_ge(S("level_out"), n)
                base = 2 * ((n + 1) % 2)
                if n < LEVELS - 1:
                    mm = 1 << n
                    for t in range(NT):
                        for h in range(HEADS):
                            for d in range(2):
                                half = 1 - d
                                o = ps[:, base + t, P * h:P * h + P].rearrange("p (b two m) -> p b two m", two=2, m=mm)
                                r = QG[:, 4 * d + h, P * t:P * t + P].rearrange("p (b two m) -> p b two m", two=2, m=mm)
                                m = pe.matmul(o[:, :, half, :], KG[:, 4 * d + h, P * t:P * t + P],
                                              r[:, :, half, :], start=True, stop=True, skip_group_check=True)
                else:
                    for h in range(HEADS):
                        for d in range(2):
                            m = pe.matmul(ps[:, base + d, P * h:P * h + P], KG[:, 4 * d + h, P * d:P * d + P],
                                          QG[:, 4 * d + h, P * (1 - d):P * (1 - d) + P], start=True, stop=True,
                                          skip_group_check=True)
                count(m, "level")
                if 2 <= n < 6:
                    i = n - 2
                    pe.wait_ge(S("kgc_ready"), 1)
                    if i >= 1:
                        pe.wait_ge(S("kt_out"), i)
                    for g in range(4):
                        m = pe.transpose(ps[:, 5, P * g:P * g + P],
                                         KGC[:, 4 * (i % 2) + g, P * (i // 2):P * (i // 2) + P], ident)
                    count(m, "kt")
                if n >= 6:
                    i = n - 6
                    pe.wait_ge(S("kt_out"), 4)
                    if i == 1:
                        pe.wait_ge(S("s0_out"), 1)
                    for g in range(4):
                        for t in range(NT):
                            m = pe.matmul(ps[:, 5, P * g:P * g + P], KT[:, t, 4 * i + g, :], VC[:, t, P * g:P * g + P],
                                          start=(t == 0), stop=(t == 1))
                    count(m, "s0")
                fill(2 if n < LEVELS - 1 else 0)
            pe.wait_ge(S("level_out"), LEVELS + 1)
            pe.wait_ge(S("s0_out"), 2)
            for h in range(HEADS):
                for t in range(NT):
                    pe.matmul(ps[:, h, 0:T], VT[:, t, P * h:P * h + P], AT[:, t, h, :], start=(t == 0), stop=False)
                for d in range(2):
                    m = pe.matmul(ps[:, h, 0:T], S0[:, 4 * d + h, :], QG[:, 4 * d + h, :], start=False, stop=(d == 1))
            count(m, "o_done")
            pe.wait_ge(S("o_squared"), 1)
            for t in range(NT):
                for h in range(HEADS):
                    m = pe.matmul(ps[:, 5, HEADS * t + h:HEADS * t + h + 1], SQ[:, h, P * t:P * t + P], ones[:, 0:1],
                                  start=True, stop=True)
            count(m, "o_summed")
            pe.wait_ge(S("o_diagonal"), 1)
            for t in range(NT):
                m = pe.matmul(ps[:, 6 + t, :], ones, ROOTS[:, HEADS * t:HEADS * t + HEADS, :], start=True, stop=True)
            count(m, "o_spread")
            dense(out1)

            todo += [(4, k) for k in range(KD)] + [(5, k) for k in range(KD)]
            sum_squares()
            fill(3)
            pe.wait_ge(S("modulated"), 3 * KD)
            for t in range(NT):
                for k in range(KD):
                    m = pe.matmul(ps[:, 5, 16 * t:16 * t + 16], H[:, k, P * t:P * t + P], WR[:, k, :],
                                  start=(k == 0), stop=(k == KD - 1))
            count(m, "logits")
            for t in range(NT):
                for k in range(KD):
                    m = pe.transpose(ps[:, 2 * t + k // 4, P * (k % 4):P * (k % 4) + P], H[:, k, P * t:P * t + P], ident)
            count(m, "h_turned")
            fill(2)
            pe.wait_ge(S("aff"), 1)
            for t in range(NT):
                m = pe.transpose(ps[0:16, 5, P * t:P * t + P], AFF[:, t, :], ident)
            count(m, "aff_turned")
            fill(3)
            pe.wait_ge(S("pos"), 1)
            for t in range(NT):
                m = pe.transpose(ps[:, 5, 16 * t:16 * t + 16], POS[0:16, P * t:P * t + P], ident[0:16, 0:16])
            count(m, "pos_turned")
            pe.wait_ge(S("sel"), 1)
            pe.wait_ge(S("h_tok"), 4)
            for c in range(KD):
                if c >= 4:
                    pe.wait_ge(S("xs_out"), c - 3)
                for t in range(NT):
                    m = pe.matmul(ps[:, c % 4, :], HTOK[:, t, P * c:P * c + P], SEL[:, t, :, :],
                                  start=(t == 0), stop=(t == NT - 1))
                count(m, "xs")
                if c % 2:
                    fill(1)
            for t in range(NT):
                pe.wait_ge(S(f"gated{t}"), 1)
            for g in range(EXPERTS // 2):
                pe.wait_ge(S("xs_out"), min(KD, g + 5))
                if g >= 4:
                    pe.wait_ge(S("pgt_out"), g - 3)
                for i in range(2):
                    for t in range(NT):
                        m = pe.transpose(ps[:, g % 4, T * i + P * t:T * i + P * t + P],
                                         PG[:, t, 2 * g + i, :], ident)
                count(m, "pgt")
            fill(16)
            pe.wait_ge(S("mod_ready"), 6)
            pe.wait_ge(S("pgt_out"), EXPERTS // 2)

            pe.sem_inc(S("scattered"), 1)
            with pe.Fori(0, EXPERTS) as e:
                pe.wait_ge(S("xcur"), e + 1)
                pe.wait_ge(S("hid_done"), e + 1)
                for k in range(16):
                    s = (exp0 + k) % RING
                    pe.wait_ge(w_ready[s], e * (16 * EXP_UNITS // RING) + plan.ready[exp0 + k])
                    for i in range(2):
                        for j in range(CG):
                            at = FJ * j + FJ // 2 * i
                            m = pe.matmul(ps[32 * j:32 * j + 32, 2 * (k // 8) + i, 0:FJ // 2], XCUR[:, k % 8, :],
                                          ring[:, s, at:at + FJ // 2], start=(k % 8 == 0), stop=(k % 8 == 7),
                                          skip_group_check=True)
                    count(m, "unit_used")
                pe.wait_ge(S("hid_t"), e + 1)
                pe.wait_ge(S("acc_done"), e + 1)
                for k in range(16, EXP_UNITS):
                    s = (exp0 + k) % RING
                    pe.wait_ge(w_ready[s], e * (16 * EXP_UNITS // RING) + plan.ready[exp0 + k])
                    c0 = 3 * (k - 16)
                    for c in range(c0, min(c0 + 3, FC)):
                        for j in range(CG):
                            at = D * (c - c0) + T * j
                            m = pe.matmul(ps[32 * j:32 * j + 32, 4, 0:T], HIDT[:, c, :], ring[:, s, at:at + T],
                                          start=(c == 0), stop=(c == FC - 1), skip_group_check=True)
                    count(m, "unit_used")
                pe.wait_ge(S("ye"), e + 1)
                pe.wait_ge(S("pgcur"), e + 1)
                for i in range(2):
                    for j in range(CG):
                        m = pe.matmul(ps[:, 4 + j, T * i:T * i + T], YE[32 * j:32 * j + 32, P * i:P * i + P],
                                      PGCUR[32 * j:32 * j + 32, :], start=True, stop=True)
                count(m, "scattered")

            sum_squares()
            sum_squares()
            rest = dense_blocks(in2, lambda it: (X_HI, X_LO), split_input())

            heads_done = [0]

            def attention(rest, units):
                for _ in range(QKV):
                    next(rest)
                def scores(h):
                    n = heads_done[0] + h
                    if h == 0:
                        pe.wait_ge(S("evacuated"), out_by(units, 11))
                    if n >= 2:
                        pe.wait_ge(S("scores_read"), n - 1)
                    r = 64 * (h % 2)
                    for t in range(NT):
                        m = pe.matmul(ps[:, 4 + n % 2, T * t:T * t + T], QA[r:r + 64, h // 2, P * t:P * t + P],
                                      KA[r:r + 64, h // 2, :], start=True, stop=True)
                    count(m, "scores")

                def turn_probs(h):
                    n = heads_done[0] + h
                    pe.wait_ge(S("probs"), n + 1)
                    if n >= 1:
                        pe.wait_ge(S("pt_out"), n)
                    for kt in range(NT):
                        for t in range(NT):
                            m = pe.transpose(ps[:, 6, T * kt + P * t:T * kt + P * t + P],
                                             SC[:, n % 2, T * t + P * kt:T * t + P * kt + P], ident)
                    count(m, "pt")

                def values(h):
                    n = heads_done[0] + h
                    pe.wait_ge(S("pt_out"), n + 1)
                    if n >= 2 and h % 2 == 0:
                        pe.wait_ge(S("ao_out"), n // 2)
                    r = 64 * (h % 2)
                    for kt in range(NT):
                        m = pe.matmul(ps[r:r + 64, 7, 0:T], VA[:, kt, 64 * h:64 * h + 64],
                                      PT[:, n % 2, T * kt:T * kt + T], start=(kt == 0), stop=(kt == 1))
                    count(m, "ao")

                scores(0)
                for h in range(ATT):
                    if h + 1 < ATT:
                        scores(h + 1)
                    for _ in range(shares(units)[h][0]):
                        next(rest)
                    turn_probs(h)
                    for _ in range(shares(units)[h][1]):
                        next(rest)
                    values(h)
                assert next(rest, 0) == 0
                heads_done[0] += ATT

            attention(rest, in2)
            pe.wait_ge(S("evacuated"), in2[-1]["items"][-1]["b"] + 1)
            pe.wait_ge(S("vsn"), 1)
            for t in range(NT):
                for g in range(ATT):
                    r = 64 * (g % 2)
                    m = pe.matmul(ps[r:r + 64, g // 2, P * t:P * t + P], VSN[:, t, 64 * g:64 * g + 64], WS[:, g, :],
                                  start=True, stop=True, skip_group_check=True)
            count(m, "sgu")
            pe.wait_ge(S("ao_out"), heads_done[0] // 2)
            for g in proj2:
                unit_ready(g["u"])
                w = slot(g["u"], 2, 4, g["w"])
                for it in g["items"]:
                    pe.wait_ge(S("evacuated"), it["b"] - 3)
                    pe.wait_ge(S("sgu_read" if it["src"] == 0 else "sgo"), 1)
                    for k in range(4):
                        m = pe.matmul(ps[:, it["b"] % 4, 0:T], w[:, it["src"], k, it["col"]:it["col"] + P],
                                      (AO, SGO)[it["src"]][:, k, :], start=(k == 0), stop=(k == 3))
                    count(m, "unit_used" if it["last"] else "block_done")
            dense(out2)
            sum_squares()
            dense(ff1)
            for g in ff2:
                for b, u in enumerate(g["us"]):
                    lo = slot(u, KD, g["w"], of=ring_lo)
                    pe.wait_ge(S("ff_split"), KD * (b + 1))
                    for it, (_, s) in zip(g["items"], g["at"][b]):
                        pe.wait_ge(S("w_split"), s + 1)
                        if b == 0:
                            pe.wait_ge(S("evacuated"), it["b"] - 3)
                        for k in range(KD):
                            wl = lo[:, k, it["col"]:it["col"] + P]
                            x = FF_HI[:, KD * b + k, :], FF_LO[:, KD * b + k, :]
                            for j, (w, a) in enumerate(parts(w_hi[:, s % HI, k, :], wl, *x)):
                                m = pe.matmul(ps[:, it["b"] % 4, 0:T], w, a, start=(b == 0 and k == 0 and j == 0),
                                              stop=(b == FF // D - 1 and k == KD - 1 and j == 2), skip_group_check=True)
                        count(m, plan.splits[s]["done"][0])
            sum_squares()
            for l in range(LAYERS3):
                sum_squares()
                rest = dense_blocks(in3[l], lambda it: (X_HI, X_LO), split_input())
                attention(rest, in3[l])
                dense(out3[l])
                sum_squares()

        @block.scalar
        def _(act):
            made = {}

            def link(ins, name):
                made[name] = made.get(name, 0) + 1
                ins.then_inc(S(name), 1)
                act.wait_ge(S(name), made[name])

            def mark(ins, name):
                made[name] = made.get(name, 0) + 1
                ins.then_inc(S(name), 1)

            def rows_out(p):
                act.wait_ge(S("unit_used"), ada[p][-1] + 1)
                if p > 0:
                    act.wait_ge(S("turned"), p)
                mark(act.activation(rows[:, :, :], ps[:, 6:8, 0:ADA_J // 2], ACT.Copy), "rows_out")

            split_next = [0]

            def high_parts(end, group_end="end"):
                while split_next[0] < min(end, starts[group_end]):
                    s = split_next[0]
                    c = plan.splits[s]
                    act.wait_ge(w_ready[c["u"] % RING], plan.ready[c["u"]])
                    if s >= HI:
                        act.wait_ge(S(plan.splits[s - HI]["done"][0]), plan.splits[s - HI]["done"][1])
                    mark(act.activation(w_hi[:, s % HI, :, :], slot(c["u"], KD, c["w"])[:, :, c["col"]:c["col"] + P],
                                        ACT.Copy), "w_high")
                    split_next[0] += 1

            group = ["out1"]

            def evacuate(it, dst, func=ACT.Copy, scale=1.0):
                if "s" in it:
                    high_parts(it["s"] + HI, group[0])
                act.wait_ge(S(it["done"][0]), it["done"][1])
                src = ps[:, it["b"] % 4, 0:T]
                if it.get("turned"):
                    src = ps[:, it["b"] % 4, :].rearrange("p (t n) -> p t n", t=NT)
                mark(act.activation(dst, src, func, scale=scale), "evacuated")

            norm_no = [0]
            root_no = [0]

            def root():
                root_no[0] += 1
                act.preload_act_table(ACT.Sqrt)
                act.wait_ge(S("mean_square"), root_no[0])
                mark(act.activation(rs[:, 0:T], rs[:, 0:T], ACT.Sqrt), "rooted")

            def modulate(dst, shift, src=XN, rooted=False, high=None):
                norm_no[0] += 1
                k = norm_no[0]
                if not rooted:
                    root()
                act.wait_ge(S("scale_ready"), k)
                a = k % 8
                for c in range(KD):
                    act.wait_ge(S("normed"), KD * (k - 1) + c + 1)
                    if shift is None:
                        mark(act.activation(dst[:, c, :], src[:, c, :], ACT.Copy, scale=scl[:, a, c:c + 1]), "scaled")
                    else:
                        mark(act.activation(dst[:, c, :], src[:, c, :], ACT.Identity, scale=scl[:, a, c:c + 1],
                                            bias=shift[:, c:c + 1]), "modulated")
                        if high is not None:
                            mark(act.activation(high[:, c, :], src[:, c, :], ACT.Identity, scale=scl[:, a, c:c + 1],
                                                bias=shift[:, c:c + 1]), "x_high")

            act.wait_ge(S("vec_in"), 16)
            act.wait_ge(S("conds_zero"), 1)
            act.activation(conds[:, :, 0:4].rearrange("p k c -> p c k"),
                           vec[:, 0:32].rearrange("p (c k) -> p c k", c=4), ACT.Silu).then_inc(S("conds_ready"), 1)
            act.wait_ge(S("lb_sub"), 1)
            mark(act.activation(small[:, 16:32], small[:, 0:16], ACT.Exp), "lb_exp")
            root()
            root()
            rows_out(0)

            def bias_row(h):
                act.wait_ge(S("brow"), h + 1)
                if h >= 2:
                    act.wait_ge(S(f"bias_stored{h % 2}"), 16 * (h // 2))
                link(act.activation(BROW[:, h % 2, 0:511], ps[:, 4 + h % 2, 0:511], ACT.Copy), "brow_out")
                act.dma_start(scratch[h:h + 1, 0:P * 512].rearrange("a (q j) -> q (a j)", q=P)[:, 0:511],
                              BROW[:, h % 2, 0:511]).then_inc(S(f"bias_stored{h % 2}"), 16)

            high_parts(starts["in1"] + 3)
            modulate(H, mod[:, 0, 0:8], rooted=True, high=X_HI)
            modulate(HC, modc[:, 0:8], src=CTX, rooted=True, high=C_HI)
            done = 0
            for g in in1:
                for it in g["items"]:
                    n, lat = it["n"], it["src"] == "lat"
                    if n < 4:
                        evacuate(it, U[:, n, :])
                    elif n < 8:
                        evacuate(it, Q[:, n - 4, :], ACT.Silu)
                    elif n < 12:
                        evacuate(it, (VT if lat else VC)[:, :, P * (n - 8):P * (n - 8) + 2 * P])
                    elif n < 20:
                        evacuate(it, (FG if lat else FGC)[:, n - 12, :], ACT.Sigmoid)
                    else:
                        evacuate(it, SG[:, n - 20, :], ACT.Silu)
                    done += 1
                    if done % BROW_EVERY == 0 and done <= ATT * BROW_EVERY:
                        bias_row(done // BROW_EVERY - 1)
            rows_out(1)
            act.wait_ge(S("dft_feat"), 1)
            mark(act.activation(ar(2 * K1, 4, 512), ps[:, 0:4, :], ACT.Copy), "dft_out")
            act.wait_ge(S("dft_tok"), 1)
            mark(act.activation(Z, ps[:, 0:4, 0:T], ACT.Copy), "z_out")
            act.wait_ge(S("fourier"), 1)
            mark(act.activation(CAT[:, 0:HEADS, :], ps[:, 0:4, 0:T], ACT.Copy), "fourier_out")
            for i in range(4):
                act.wait_ge(S("kt"), i + 1)
                k = 4 * (i % 2)
                mark(act.activation(KT[:, i // 2, k:k + 4, :], ps[:, 5, :].rearrange("p (g d) -> p g d", g=4),
                                    ACT.Copy), "kt_out")
                if i == 0:
                    rows_out(2)
            for i in range(2):
                act.wait_ge(S("s0"), i + 1)
                mark(act.activation(S0[:, 4 * i:4 * i + 4, :], ps[:, 5, :].rearrange("p (g d) -> p g d", g=4),
                                    ACT.Copy), "s0_out")
                if i == 0:
                    rows_out(3)
            group[0] = "in2"
            high_parts(starts["out1"] + 3)
            act.preload_act_table(ACT.Sqrt)
            act.wait_ge(S("o_mean"), 1)
            mark(act.activation(rs[:, 0:NT * HEADS], rs[:, 0:NT * HEADS], ACT.Sqrt), "o_rooted")
            for g in out1:
                for it in g["items"]:
                    evacuate(it, SQ[:, it["n"], :], ACT.Copy, mod[:, 0, 16 + it["n"]:17 + it["n"]])
            modulate(H, mod[:, 1, 0:8])
            act.wait_ge(S("h_turned"), 1)
            for t in range(NT):
                for i in range(2):
                    mark(act.activation(HTOK[:, t, 512 * i:512 * i + 512], ps[:, 2 * t + i, :], ACT.Copy), "h_tok")
            act.wait_ge(S("logit_max"), 1)
            for t in range(NT):
                mark(act.activation(AFF[:, t, :], AFF[:, t, :], ACT.Exp, bias=small[:, 40 + t:41 + t],
                                    accum_out=small[:, 42 + t:43 + t]), "aff_exp")
            rows_out(4)
            for c in range(KD):
                act.wait_ge(S("xs"), c + 1)
                mark(act.activation(XS[:, c, :], ps[:, c % 4, :], ACT.Copy), "xs_out")
            for g in range(EXPERTS // 2):
                act.wait_ge(S("pgt"), g + 1)
                mark(act.activation(PGT[:, 2 * g:2 * g + 2, :], ps[:, g % 4, :].rearrange("p (e t) -> p e t", e=2),
                                    ACT.Copy), "pgt_out")
            rows_out(5)
            act.wait_ge(S("sel"), 1)
            act.dma_start(WS, inp["w_sgu"]).then_inc(S("sgu_in"), 16)
            act.dma_start(GS, inp["g_sgu"]).then_inc(S("sgu_in"), 16)
            act.dma_start(BS, inp["b_sgu"]).then_inc(S("sgu_in"), 16)

            with act.Fori(0, EXPERTS) as e:
                act.wait_ge(S("unit_used"), e * EXP_UNITS + (exp0 + 8))
                act.wait_ge(S("hid_done"), e + 1)
                act.activation(SIL, ps[:, 0:2, 0:FJ // 2], ACT.Silu).then_inc(S("sil"), 1)
                act.wait_ge(S("unit_used"), e * EXP_UNITS + (exp0 + EXP_UNITS))
                act.wait_ge(S("scattered"), e + 1)
                act.activation(YE, ps[:, 4, 0:T], ACT.Copy).then_inc(S("ye"), 1)

            act.wait_ge(S("acc_done"), EXPERTS + 1)
            group[0] = "out2"
            high_parts(starts["in2"] + 3)
            modulate(X, None)
            modulate(H, mod[:, 2, 0:8], high=X_HI)
            def in2_out():
                for it in [it for g in in2 for it in g["items"]]:
                    n = it["n"]
                    if n < 4:
                        evacuate(it, QA[:, n, :], ACT.Copy, 0.125)
                    elif n < 8:
                        evacuate(it, KA[:, n - 4, :])
                    elif n < 12:
                        evacuate(it, VA[:, :, P * (n - 8):P * (n - 8) + 2 * P])
                    elif n < 16:
                        evacuate(it, UA[:, n - 12, :], ACT.Gelu_apprx_tanh)
                    elif n < 20:
                        evacuate(it, VS[:, :, P * (n - 16):P * (n - 16) + 2 * P], ACT.Gelu_apprx_tanh)
                    elif n < 28:
                        evacuate(it, GA[:, n - 20, :], ACT.Sigmoid)
                    else:
                        evacuate(it, GB[:, n - 28, :], ACT.Sigmoid)
                    yield

            def gating_norm(h):
                if h == 3:
                    act.wait_ge(S("evacuated"), out_by(in2, 19))
                    for t in range(NT):
                        link(act.activation(SQ[:, 2 * t:2 * t + 2, :], VS[:, t, :].rearrange("p (a b) -> p a b", a=2),
                                            ACT.Square, accum_out=small[:, 44 + t:45 + t]), "vs_sq")
                if h == 5:
                    act.wait_ge(S("vs_mean"), 1)
                    mark(act.activation(small[:, 44:46], small[:, 44:46], ACT.Sqrt), "vs_rooted")

            heads = [0]

            def softmax_exp(rest, units, between=lambda h: None):
                def exp(n):
                    act.wait_ge(S("row_max"), n + 1)
                    for t in range(NT):
                        mark(act.activation(SC[:, n % 2, T * t:T * t + T], SC[:, n % 2, T * t:T * t + T], ACT.Exp,
                                            bias=small[:, 48 + 2 * (n % 2) + t:49 + 2 * (n % 2) + t],
                                            accum_out=small[:, 52 + 2 * (n % 2) + t:53 + 2 * (n % 2) + t]), "p_exp")

                for _ in range(QKV):
                    next(rest)
                n0 = heads[0]
                exp(n0)
                for n in range(n0, n0 + ATT):
                    if n + 1 < n0 + ATT:
                        exp(n + 1)
                    for _ in range(shares(units)[n - n0][0]):
                        next(rest)
                    act.wait_ge(S("pt"), n + 1)
                    if n >= 2:
                        act.wait_ge(S("ao"), n - 1)
                    mark(act.activation(PT[:, n % 2, :], ps[:, 6, :], ACT.Copy), "pt_out")
                    for _ in range(shares(units)[n - n0][1]):
                        next(rest)
                    between(n - n0)
                heads[0] += ATT

            softmax_exp(in2_out(), in2, gating_norm)
            group[0] = "end"
            for g in proj2:
                for it in g["items"]:
                    evacuate(it, (SQ, XN)[it["src"]][:, it["n"], :])
            high_parts(starts["out2"] + 3)
            for g in out2:
                for it in g["items"]:
                    evacuate(it, SQ[:, it["n"], :], ACT.Copy, mod[:, 2, 16 + it["n"]:17 + it["n"]])
            modulate(H, mod[:, 3, 0:8], high=X_HI)
            for g in ff1:
                for it in g["items"]:
                    evacuate(it, HFF[:, it["n"], :], ACT.Relu)
            for g in ff2:
                for at in g["at"]:
                    for it, s in at:
                        high_parts(s + HI)
                        if it is not None:
                            evacuate(it, SQ[:, it["n"], :], ACT.Copy, mod[:, 3, 16 + it["n"]:17 + it["n"]])
            for i in range(2):
                act.wait_ge(S(f"bias_stored{i}"), 16 * ATT // 2)
            for t in range(NT):
                at = T - 1 - P * t
                view = scratch[:, at:at + P * 511].rearrange("h (q j) -> q h j", j=511)
                act.dma_start(BIAS[:, :, T * t:T * t + T], view[:, :, 0:T]).then_inc(S("bias_in"), 16)
            modulate(X, None)
            for l in range(LAYERS3):
                modulate(H, mod[:, 4 + l, 0:8], high=X_HI)

                def in3_out():
                    for it in [it for g in in3[l] for it in g["items"]]:
                        n = it["n"]
                        if n < 4:
                            evacuate(it, QA[:, n, :], ACT.Copy, 0.125)
                        elif n < 8:
                            evacuate(it, KA[:, n - 4, :])
                        elif n < 12:
                            evacuate(it, VA[:, :, P * (n - 8):P * (n - 8) + 2 * P])
                        else:
                            q = (n - 12) // 4
                            evacuate(it, (HQ, CU, CB, CC, CS)[q][:, n % 4, :], ACT.Silu if q in (0, 4) else ACT.Copy)
                        yield

                softmax_exp(in3_out(), in3[l])
                for g in out3[l]:
                    for it in g["items"]:
                        evacuate(it, MIX3[:, it["n"], :])
                modulate(SQ, None)

        @block.vector
        def _(dve):
            made = {}

            def link(ins, name="dve_step"):
                made[name] = made.get(name, 0) + 1
                ins.then_inc(S(name), 1)
                dve.wait_ge(S(name), made[name])

            def waits(name, n):
                dve.wait_ge(S(name), n)

            tt, ts, stt = dve.tensor_tensor, dve.tensor_scalar, dve.scalar_tensor_tensor
            norms = [0]

            before = []
            modulations = {"modulated": 0, "scaled": 0}
            squares = [0]

            def square(c, src):
                link(tt(SQ[:, c, :], src[:, c, :], src[:, c, :], ALU.mult), "squared")

            def normalise(src, dst=XN, then=lambda c: None):
                norms[0] += 1
                k = norms[0]
                if before:
                    waits(*before.pop())
                waits("summed", k)
                r = rs[:, 0:T]
                link(ts(r, ps[:, 5, 0:T], 1.0 / D, EPS, ALU.mult, ALU.add), "mean_square")
                waits("rooted", k)
                link(dve.reciprocal(r, r))
                for c in range(KD + 2):
                    if c < KD:
                        link(tt(dst[:, c, :], src[:, c, :], r, ALU.mult), "normed")
                    if c >= 2:
                        then(c - 2)

            split_no = [0]

            def low(x, hi, lo, c, k=1):
                for i in range(c, c + k):
                    link(tt(lo[:, i, :], x[:, i, :], hi[:, i, :].bitcast(F32), ALU.subtract), "x_split")

            def low_modulated(c, x=H, hi=X_HI, lo=X_LO):
                split_no[0] += 1
                waits("x_high", split_no[0])
                low(x, hi, lo, c)

            def split(x, c, k=1):
                link(dve.tensor_copy(X_HI[:, c:c + k, :], x[:, c:c + k, :]))
                low(x, X_HI, X_LO, c, k)

            scales = [0]

            def scale_columns(gain, plus_one=None, times=None):
                scales[0] += 1
                a = scl[:, scales[0] % 8, :]
                if times is not None:
                    link(tt(a, gain, times, ALU.mult), "scale_ready")
                elif plus_one is None:
                    link(dve.tensor_copy(a, gain), "scale_ready")
                else:
                    link(stt(a, plus_one, 1.0, gain, ALU.add, ALU.mult), "scale_ready")

            def rms(src, gain, plus_one=None, times=None, by="modulated", then=lambda c: None):
                scale_columns(gain, plus_one, times)
                modulations[by] += KD
                normalise(src, then=then)
                before.append((by, modulations[by]))

            def final_square(c):
                waits("scaled", modulations["scaled"] - KD + c + 1)
                square(c, X)

            def mod_in(p):
                waits("turned", p + 1)
                bias = [V("b_ada", 0, 24), V("b_ada", 24, 24), V("b_ada_2", 0, 24), V("b_ada_2", 24, 24),
                        V("b_ada_3", 0, 24), V("b_ada_3", 24, 24)][p]
                v = ps[:, 4, 0:96].rearrange("p (q j c) -> p j q c", q=6, j=CG)
                bias = bias.rearrange("p (j q) -> p j q", j=CG)
                if p == 0:
                    link(tt(modc[:, :].rearrange("p (j q) -> p j q", j=CG), v[:, :, :, 1], bias, ALU.add))
                link(tt(mod[:, p, :].rearrange("p (j q) -> p j q", j=CG), v[:, :, :, (0, 0, 2, 2, 3, 3)[p]], bias,
                        ALU.add), "mod_ready")

            def residual(units):
                for g in units:
                    for it in g["items"]:
                        waits("evacuated", it["b"] + 1)
                        link(tt(X[:, it["n"], :], X[:, it["n"], :], SQ[:, it["n"], :], ALU.add))
                        square(it["n"], X)

            link(dve.memset(conds[:], 0.0), "conds_zero")
            waits("vec_in", 16)
            waits("small_in", 16)
            lg = V("lb_logits", 0, 16)
            link(tt(small[:, 32:40], lg[:, 0:8], lg[:, 8:16], ALU.max))
            link(tt(small[:, 0:8], lg[:, 0:8], small[:, 32:40], ALU.subtract))
            link(tt(small[:, 8:16], lg[:, 8:16], small[:, 32:40], ALU.subtract), "lb_sub")
            waits("x_in", 32)
            for c in range(KD):
                square(c, X)
            waits("rel_in", 32)
            link(dve.tensor_copy(RELB[0:33, :, :], REL[0:33, :].unsqueeze(2).broadcast_to([33, ATT, P])), "relb")
            waits("lb_exp", 1)
            link(tt(small[:, 32:40], small[:, 16:24], small[:, 24:32], ALU.add))
            link(dve.reciprocal(small[:, 40:48], small[:, 32:40]))
            link(tt(small[:, 0:8], small[:, 16:24], small[:, 40:48], ALU.mult))
            link(ts(small[:, 8:16], small[:, 0:8], -1.0, 1.0, ALU.mult, ALU.add), "lb_ready")
            normalise(X)
            for c in range(KD):
                square(c, CTX)
            normalise(CTX, CTX)
            mod_in(0)
            scale_columns(V("g_mix", 0, 8), mod[:, 0, 8:16])
            scale_columns(V("g_mix", 0, 8), modc[:, 8:16])
            modulations["modulated"] = 2 * KD
            for parts in ((H, X_HI, X_LO), (HC, C_HI, C_LO)):
                for c in range(KD):
                    low_modulated(c, *parts)

            waits("evacuated", in1[-1]["items"][-1]["b"] + 1)
            link(dve.memset(AT, 0.0))
            for g in range(8):
                link(ts(FG[:, g, :], FG[:, g, :], small[:, 8 + g:9 + g], small[:, g:g + 1], ALU.mult, ALU.add))
            link(ts(KG, FG, -1.0, 1.0, ALU.mult, ALU.add))
            for d in range(2):
                link(tt(QG[:, 4 * d:4 * d + 4, :], Q, FG[:, 4 * d:4 * d + 4, :], ALU.mult),
                     "qk_first" if d == 0 else "kg_ready")
            mod_in(1)

            waits("const_in", 16)

            def level_out(n, level):
                waits("level", n + 1)
                base = 2 * (n % 2)
                if level < LEVELS:
                    mask = C("levels")[:, P * level:P * level + P].bitcast(I32)
                    for t in range(NT):
                        link(dve.copy_predicated(AT[:, t, :, P * t:P * t + P],
                                                 mask.unsqueeze(1).broadcast_to([P, HEADS, P]),
                                                 ps[:, base + t, :].rearrange("p (h x) -> p h x", h=HEADS)),
                             "dve_step" if t == 0 else "level_out")
                else:
                    for d in range(2):
                        link(dve.tensor_copy(AT[:, d, :, P * (1 - d):P * (1 - d) + P],
                                             ps[:, base + d, :].rearrange("p (h x) -> p h x", h=HEADS)),
                             "dve_step" if d == 0 else "level_out")

            cur = FG.rearrange("p g t -> p (g t)")
            nxt = [TA, TB]
            for n in range(LEVELS):
                level_out(n, LEVELS - 1 if n == 0 else n - 1)
                waits("level", n + 2)
                m = 1 << n

                def halves(a, d):
                    return a[:, 4 * d:4 * d + 4, :].rearrange("p g (b two m) -> p (g b) two m", two=2, m=m)

                nb = T // m
                pair = cur[:, 0:8 * nb].rearrange("p (x two) -> p x two", two=2)
                for a, side in ((KG, 0), (QG, 1)) if n < LEVELS - 1 else ((QG, 1),):
                    for d in range(2):
                        s = side ^ d
                        v = halves(a, d)[:, :, s, :]
                        tot = pair[:, 2 * nb * d:2 * nb * d + 2 * nb, 1 - s]
                        link(tt(v, v, tot.unsqueeze(2).broadcast_to([P, 2 * nb, m]), ALU.mult),
                             "qk_ready" if a is QG and d == 1 else "dve_step")
                if n < LEVELS - 1:
                    o = nxt[n % 2][:, 0:4 * nb]
                    link(tt(o, pair[:, :, 0], pair[:, :, 1], ALU.mult))
                    cur = o
                if n in (5, 7):
                    mod_in(n // 2)
            level_out(LEVELS, LEVELS)

            waits("fourier_out", 1)
            split(CAT, 0, HEADS)
            waits("o_done", 1)
            O = ar(K1, HEADS, T)
            link(dve.tensor_copy(O, ps[:, 0:4, 0:T]))
            link(tt(SQ[:, 0:4, :], O, O, ALU.mult), "o_squared")
            waits("o_summed", 1)
            root = rs[:, 0:NT * HEADS]
            link(ts(root, ps[:, 5, 0:NT * HEADS], 1.0 / P, EPS, ALU.mult, ALU.add), "o_mean")
            waits("o_rooted", 1)
            link(dve.reciprocal(root, root))
            full = [P, NT * HEADS, P]
            link(tt(ROOTS, ident.unsqueeze(1).broadcast_to(full), root.unsqueeze(2).broadcast_to(full), ALU.mult),
                 "o_diagonal")
            waits("o_spread", 1)
            o = O.rearrange("p h (t x) -> p t h x", t=NT)
            link(tt(o, o, ps[:, 6:8, :].rearrange("p t (h x) -> p t h x", h=HEADS), ALU.mult))
            for h in range(HEADS):
                link(stt(CAT[:, HEADS + h, :], O[:, h, :], V("g_rec", h), SG[:, h, :], ALU.mult, ALU.mult))
                split(CAT, HEADS + h)
            residual(out1)
            rms(X, V("g_ffn", 0, 8), mod[:, 1, 8:16])

            waits("logits", 1)
            lgt = ps[:, 5, 0:32].rearrange("p (t e) -> p t e", t=NT)
            waits("modulated", 3 * KD)
            link(dve.tensor_copy(AFF, lgt), "logits_read")
            link(dve.tensor_reduce(small[:, 38:40], AFF, AX_X, ALU.max))
            link(ts(small[:, 40:42], small[:, 38:40], -1.0, None, ALU.mult), "logit_max")
            waits("aff_exp", 2)
            link(dve.reciprocal(small[:, 38:40], small[:, 42:44]))
            for t in range(NT):
                link(ts(AFF[:, t, :], AFF[:, t, :], small[:, 38 + t:39 + t], None, ALU.mult),
                     "dve_step" if t == 0 else "aff")
            waits("aff_turned", 1)
            work, mask, pos, one = WORK[0:16, :], MASK[0:16, :], POS[0:16, :], ONE[0:16, :]
            link(dve.tensor_copy(work, ps[0:16, 5, 0:T]))
            link(dve.memset(one, 1.0))
            for _ in range(SLOTS // 8):
                link(dve.max(small[0:16, 0:8], work))
                link(dve.match_replace(work, small[0:16, 0:8], work, -1.0))
            link(ts(mask, work, 0.0, None, ALU.is_lt))
            link(dve.tensor_tensor_scan(pos, one, mask, 0.0, ALU.mult, ALU.add))
            link(tt(pos, pos, mask, ALU.mult), "pos")
            mod_in(4)
            waits("pos_turned", 1)
            link(dve.tensor_copy(POST, ps[:, 5, 0:32].rearrange("p (t e) -> p t e", t=NT)))
            for t in range(NT):
                link(tt(SEL[:, t, :, :], POST[:, t, :].unsqueeze(2).broadcast_to([P, EXPERTS, SLOTS]),
                        C("slots").unsqueeze(1).broadcast_to([P, EXPERTS, SLOTS]), ALU.is_equal),
                     "dve_step" if t == 0 else "sel")
            gate_selection(dve, 0)
            mod_in(5)
            link(dve.memset(MOE, 0.0), "acc_done")
            dve.sem_inc(S("hid_done"), 1)

            moe = MOE.rearrange("p (j i) t -> p j (i t)", j=CG)
            with dve.Fori(0, EXPERTS) as e:
                waits("sil", e + 1)
                waits("unit_used", e * EXP_UNITS + (exp0 + 16))
                tt(HID.rearrange("p (i f) -> p i f", i=2), SIL, ps[:, 2:4, 0:FJ // 2], ALU.mult).then_inc(S("hid_done"), 1)
                waits("hid_done", e + 2)
                dve.transpose(HIDT, HID.rearrange("p (q c) -> p c q", c=FC)).then_inc(S("hid_t"), 1)
                waits("scattered", e + 2)
                tt(moe, moe, ps[:, 4:8, :], ALU.add).then_inc(S("acc_done"), 1)
                waits("acc_done", e + 2)

            for c in range(KD):
                link(stt(X[:, c, :], MOE[:, c, :], mod[:, 1, 16 + c:17 + c], X[:, c, :], ALU.mult, ALU.add))
                square(c, X)
            rms(X, V("g_final", 0, 8), by="scaled", then=final_square)
            rms(X, V("g_mix_2", 0, 8), mod[:, 2, 8:16], then=low_modulated)

            waits("sgu_in", 48)
            link(tt(WS, WS, C("tri").unsqueeze(1).broadcast_to([P, ATT, P]), ALU.mult))

            def gating_values(h):
                if h == 4:
                    waits("vs_sq", 2)
                    link(ts(small[:, 44:46], small[:, 44:46], 1.0 / 512, EPS, ALU.mult, ALU.add), "vs_mean")
                if h == 6:
                    waits("vs_rooted", 1)
                    link(dve.reciprocal(small[:, 44:46], small[:, 44:46]))
                    for t in range(NT):
                        link(stt(VSN[:, t, :], VS[:, t, :], small[:, 44 + t:45 + t], GS, ALU.mult, ALU.mult),
                             "dve_step" if t == 0 else "vsn")

            heads = [0]

            def softmax(bias, ao_out, between=lambda h: None):
                def max_of(h):
                    n = heads[0] + h
                    waits("scores", n + 1)
                    if n >= 2:
                        waits("pt", n - 1)
                    s, b = SC[:, n % 2, :], 2 * (n % 2)
                    link(tt(s, ps[:, 4 + n % 2, :], bias(h), ALU.add), "scores_read")
                    link(dve.tensor_reduce(small[:, 56 + b:58 + b], s.rearrange("p (t k) -> p t k", t=NT), AX_X, ALU.max))
                    link(ts(small[:, 48 + b:50 + b], small[:, 56 + b:58 + b], -1.0, None, ALU.mult), "row_max")

                def divide(h):
                    n = heads[0] + h
                    b = 2 * (n % 2)
                    waits("p_exp", NT * (n + 1))
                    link(dve.reciprocal(small[:, 56 + b:58 + b], small[:, 52 + b:54 + b]))
                    for t in range(NT):
                        s = SC[:, n % 2, T * t:T * t + T]
                        link(ts(s, s, small[:, 56 + b + t:57 + b + t], None, ALU.mult), "dve_step" if t == 0 else "probs")

                def pair_out(c):
                    waits("ao", heads[0] + 2 * c + 2)
                    link(ao_out(c), "ao_out")

                max_of(0)
                for h in range(ATT):
                    if h + 1 < ATT:
                        max_of(h + 1)
                    divide(h)
                    between(h)
                    if h >= 2 and h % 2 == 0:
                        pair_out(h // 2 - 1)
                pair_out(ATT // 2 - 1)
                heads[0] += ATT

            softmax(lambda h: C("causal"), lambda c: dve.tensor_copy(AO[:, c, :], ps[:, 7, 0:T]),
                    gating_values)
            waits("sgu", 1)
            link(tt(SGO.rearrange("p c (t x) -> p c t x", t=NT), ps[:, 0:4, 0:T].rearrange("p c (t x) -> p c t x", t=NT),
                    BS.unsqueeze(2).broadcast_to([P, 4, NT, P]), ALU.add), "sgu_read")
            link(tt(SGO, SGO, UA, ALU.mult), "sgo")
            for g in proj2:
                for it in g["items"]:
                    waits("evacuated", it["b"] + 1)
                    n = it["n"]
                    if it["src"] == 0:
                        link(tt(GA[:, n, :], GA[:, n, :], SQ[:, n, :], ALU.mult))
                    else:
                        link(tt(GB[:, n, :], GB[:, n, :], XN[:, n, :], ALU.mult))
                        link(tt(MG[:, n, :], GA[:, n, :], GB[:, n, :], ALU.add))
                        split(MG, n)
            residual(out2)
            rms(X, V("g_ffn_2", 0, 8), mod[:, 3, 8:16], then=low_modulated)
            for g in ff1:
                for it in g["items"]:
                    waits("evacuated", it["b"] + 1)
                    h = HFF[:, it["n"], :]
                    link(tt(h, h, h, ALU.mult))
                    link(dve.tensor_copy(FF_HI[:, it["n"], :], h))
                    link(tt(FF_LO[:, it["n"], :], h, FF_HI[:, it["n"], :].bitcast(F32), ALU.subtract), "ff_split")
            residual(ff2)
            rms(X, V("g_final_2", 0, 8), by="scaled", then=final_square)
            for l in range(LAYERS3):
                rms(X, V("pre_norm_g_3", 8 * l, 8), mod[:, 4 + l, 8:16], then=low_modulated)
                waits("bias_in", 32)

                def convolve(h):
                    if h < ATT - 2:
                        return
                    if h == ATT - 2:
                        waits("zp_zero", 1)
                        waits("evacuated", out_by(in3[l], 27))
                        link(tt(ZP[:, :, 1:T + 1], CC, CU, ALU.mult))
                    for c in (0, 1) if h == ATT - 2 else (2, 3):
                        w = [V("conv_w_3", 12 * l + 4 * k + c) for k in range(3)]
                        y = CAT3[:, 4 + c, :]
                        link(ts(y, ZP[:, c, 0:T], w[0], None, ALU.mult))
                        for k in (1, 2):
                            link(stt(y, ZP[:, c, k:k + T], w[k], y, ALU.mult, ALU.add))
                        link(tt(y, y, CB[:, c, :], ALU.mult))

                softmax(lambda h: BIAS[:, h, :],
                        lambda c: tt(CAT3[:, c, :], ps[:, 7, 0:T], HQ[:, c, :], ALU.mult), convolve)
                waits("evacuated", out_by(in3[l], 31))
                split(CAT3, 0, 4)
                for c in range(4):
                    link(tt(CAT3[:, 4 + c, :], CAT3[:, 4 + c, :], CS[:, c, :], ALU.mult))
                    split(CAT3, 4 + c)
                for g in out3[l]:
                    for it in g["items"]:
                        waits("evacuated", it["b"] + 1)
                        square(it["n"], MIX3)

                def add_mixer(c):
                    waits("scaled", (2 + l) * KD + c + 1)
                    link(tt(X[:, c, :], X[:, c, :], SQ[:, c, :], ALU.add), "x_final" if l == LAYERS3 - 1 else "dve_step")
                    if l < LAYERS3 - 1:
                        square(c, X)

                rms(MIX3, V("post_norm_g_3", 8 * l, 8), times=mod[:, 4 + l, 16:24], by="scaled", then=add_mixer)

        @block.gpsimd
        def _(pool):
            made = {}

            def link(ins, name="pool_step"):
                made[name] = made.get(name, 0) + 1
                ins.then_inc(S(name), 1)
                pool.wait_ge(S(name), made[name])

            split_next = [0]

            def low_parts(end):
                while split_next[0] < end:
                    s = split_next[0]
                    c = plan.splits[s]
                    at = slice(c["col"], c["col"] + P)
                    pool.wait_ge(S("w_high"), s + 1)
                    pool.tensor_tensor(slot(c["u"], KD, c["w"], of=ring_lo)[:, :, at], slot(c["u"], KD, c["w"])[:, :, at],
                                       w_hi[:, s % HI, :, :].bitcast(F32), ALU.subtract).then_inc(S("w_split"), 1)
                    split_next[0] += 1

            low_parts(starts["out1"])
            pool.wait_ge(S("lb_ready"), 1)
            pool.wait_ge(S("evacuated"), in1[-1]["items"][-1]["b"] + 1)
            for g in range(8):
                link(pool.tensor_scalar(FGC[:, g, :], FGC[:, g, :], small[:, 8 + g:9 + g], small[:, g:g + 1],
                                        ALU.mult, ALU.add))
            link(pool.tensor_scalar(KGC, FGC, -1.0, 1.0, ALU.mult, ALU.add))
            cur = FGC.rearrange("p g t -> p (g t)")
            nxt = [TAC, TBC]
            for n in range(LEVELS):
                m = 1 << n
                nb = T // m
                pair = cur[:, 0:8 * nb].rearrange("p (x two) -> p x two", two=2)
                for d in range(2):
                    v = KGC[:, 4 * d:4 * d + 4, :].rearrange("p g (b two m) -> p (g b) two m", two=2, m=m)[:, :, d, :]
                    tot = pair[:, 2 * nb * d:2 * nb * d + 2 * nb, 1 - d]
                    link(pool.tensor_tensor(v, v, tot.unsqueeze(2).broadcast_to([P, 2 * nb, m]), ALU.mult),
                         "kgc_ready" if n == LEVELS - 1 and d == 1 else "pool_step")
                if n < LEVELS - 1:
                    o = nxt[n % 2][:, 0:4 * nb]
                    link(pool.tensor_tensor(o, pair[:, :, 0], pair[:, :, 1], ALU.mult))
                    cur = o
            low_parts(starts["in2"])
            pool.wait_ge(S("sel"), 1)
            gate_selection(pool, 1)
            pool.wait_ge(S("xs_out"), KD)
            pool.wait_ge(S("pgt_out"), EXPERTS // 2)
            xs = XS.rearrange("p k (e s) -> p k e s", e=EXPERTS)
            with pool.Fori(0, EXPERTS) as e:
                pool.wait_ge(S("unit_used"), e * EXP_UNITS + (exp0 - 8))
                pool.tensor_copy(XCUR, xs[:, :, e, :]).then_inc(S("xcur"), 1)
                pool.wait_ge(S("scattered"), e + 1)
                pool.tensor_copy(PGCUR, PGT[:, e, :]).then_inc(S("pgcur"), 1)
            low_parts(in3[0][0]["items"][0]["s"] + 2)
            pool.wait_ge(S("evacuated"), out_by(in3[0], 0))
            link(pool.memset(ZP, 0.0), "zp_zero")
            low_parts(starts["end"])



def kernel(**inputs):
    import concourse.bacc as _bacc
    from concourse.bass_utils import run_bass_kernel_spmd as _run

    a = {k: np.asarray(v) for k, v in inputs.items()}

    def feature_major(x):
        return np.ascontiguousarray(x.reshape(T, KD, P).transpose(2, 1, 0))

    names = {n: n for n, _ in VECTORS}
    vec = np.concatenate([a[n].reshape(-1, P).T for n in names], 1)
    const, offsets = constants()
    arrays = {
        "xT": feature_major(a["x"]), "ctxT": feature_major(a["ctx"]),
        "vec": np.ascontiguousarray(vec), "const": const, "offsets": offsets,
        "rel": np.concatenate([a["rel_bias_3"], np.ones((1, ATT), np.float32)], 0),
        "w_sgu": np.ascontiguousarray(a["w_sgu_2"][0].transpose(2, 0, 1)),
        "g_sgu": np.ascontiguousarray(np.broadcast_to(a["g_sgu_2"], (P, 512))),
        "b_sgu": np.ascontiguousarray(np.repeat(a["b_sgu_2"][0].reshape(4, 2, 1, P), 64, 2).reshape(4, P, P)
                                      .transpose(1, 0, 2)),
    }
    for n in ("w_ada", "w_in", "w_fourier", "w_out", "w_router", "w_exp_gate", "w_exp_up", "w_exp_down", "w_ada_2",
              "w_in_2", "w_proj_attn_2", "w_proj_sgu_2", "w_out_2", "w_ff1_2", "w_ff2_2", "w_ada_3", "w_in_3",
              "w_out_3"):
        arrays[n] = np.ascontiguousarray(a[n])
    nc = _bacc.Bacc("TRN2", target_bir_lowering=False, num_devices=1)
    inp = {n: nc.dram_tensor("in_" + n, v.shape, mybir.dt.from_np(v.dtype), kind="ExternalInput").ap()
           for n, v in arrays.items()}
    scratch = nc.dram_tensor("bias_rows", (ATT, 129 * 512), F32).ap()
    out = nc.dram_tensor("out_xT", (P, KD, T), F32, kind="ExternalOutput").ap()
    build(nc, inp, scratch, out)
    r = _run(nc, [{"in_" + n: v for n, v in arrays.items()}], core_ids=[0])
    return np.ascontiguousarray(r.results[0]["out_xT"].transpose(2, 1, 0).reshape(1, T, D))
```
